# Optimizing a Trainium2 kernel written in Bass

```python
import math
import jax, jax.numpy as jnp
from jax import lax
import numpy as np

D_MODEL = 1024
BATCH = 1
SEQ = 512
DEPTH = 1

D_MIX = D_MODEL
D_POOL = D_MIX // 2
POOL_WINDOWS = (2, 4, 8, 16)
N_POOL_GROUPS = len(POOL_WINDOWS)
POOL_GROUP = D_POOL // N_POOL_GROUPS
D_GMLP = D_MIX - D_POOL
N_GMLP_HEADS = 8
GMLP_HEAD = D_GMLP // N_GMLP_HEADS
CHUNK = 128
D_FF = 2816
N_SUB = 3
N_MOD = 3
EPS = 1e-6
HALF_STEP = 0.5

kernel_name = "hybrid_pool_gmlp_macaron_adaln"

def rms_norm(x, g):
    xf = x.astype(jnp.float32)
    r = lax.rsqrt(jnp.mean(xf * xf, axis=-1, keepdims=True) + EPS)
    return (xf * r).astype(x.dtype) * g

def layer_norm(x, g, b):
    xf = x.astype(jnp.float32)
    mu = jnp.mean(xf, axis=-1, keepdims=True)
    var = jnp.mean(jnp.square(xf - mu), axis=-1, keepdims=True)
    return ((xf - mu) * lax.rsqrt(var + EPS)).astype(x.dtype) * g + b

def modulate(h, shift, scale):
    return h * (1.0 + scale[:, None, :]) + shift[:, None, :]

def swiglu(h, w_in, w_out):
    gu = h @ w_in
    g, u = jnp.split(gu, 2, axis=-1)
    return (jax.nn.silu(g) * u) @ w_out

def causal_multiscale_pool(xp, w_pool, pool_scale):
    B, S, _ = xp.shape
    xg = xp.reshape(B, S, N_POOL_GROUPS, POOL_GROUP)
    xf = xg.astype(jnp.float32)
    cs = jnp.cumsum(xf, axis=1)
    pos = jnp.arange(S, dtype=jnp.int32)
    outs = []
    for i, w in enumerate(POOL_WINDOWS):
        c_i = cs[:, :, i]
        c_prev = jnp.pad(c_i[:, :-w], ((0, 0), (w, 0), (0, 0)))
        cnt = jnp.minimum(pos + 1, w).astype(jnp.float32)[None, :, None]
        outs.append((c_i - c_prev) / cnt - xf[:, :, i])
    pooled = jnp.stack(outs, axis=2).astype(xp.dtype)
    mixed = jnp.einsum('bsgc,gcd->bsgd', pooled, w_pool)
    return mixed.reshape(B, S, D_POOL) * pool_scale

def chunked_spatial_gating(zb, ln_g, ln_b, w_spatial, b_spatial):
    B, S, _ = zb.shape
    z = jax.nn.gelu(zb)
    u, v = jnp.split(z, 2, axis=-1)
    v = layer_norm(v, ln_g, ln_b)
    vc = v.reshape(B, S // CHUNK, CHUNK, N_GMLP_HEADS, GMLP_HEAD)
    mask = jnp.tril(jnp.ones((CHUNK, CHUNK), dtype=bool))
    ws = jnp.where(mask[None], w_spatial, jnp.zeros((), w_spatial.dtype))
    sv = jnp.einsum('hts,bnshc->bnthc', ws, vc)
    sv = sv + jnp.transpose(b_spatial)[None, None, :, :, None]
    return u * sv.reshape(B, S, D_GMLP)

def setup_inputs(seed: int = 0) -> dict:
    key = jax.random.key(seed)
    ks = jax.random.split(key, 24)
    f32 = jnp.float32
    L, D = DEPTH, D_MODEL

    def nrm(k, shape, fan_in):
        return jax.random.normal(k, shape, f32) * (fan_in ** -0.5)

    def gain(k, shape):
        return 1.0 + 0.05 * jax.random.normal(k, shape, f32)

    return {
        "x": jax.random.normal(ks[0], (BATCH, SEQ, D), f32),
        "c": jax.random.normal(ks[1], (BATCH, D), f32),
        "w_ada": nrm(ks[2], (L, D, N_SUB * N_MOD * D), D),
        "b_ada": 0.02 * jax.random.normal(ks[3], (L, N_SUB * N_MOD * D), f32),
        "norm_ffn1_g": gain(ks[4], (L, D)),
        "ffn1_w_in": nrm(ks[5], (L, D, 2 * D_FF), D),
        "ffn1_w_out": nrm(ks[6], (L, D_FF, D), D_FF),
        "norm_mix_g": gain(ks[7], (L, D)),
        "w_mix_in": nrm(ks[8], (L, D, D_POOL + 2 * D_GMLP), D),
        "w_pool": nrm(ks[9], (L, N_POOL_GROUPS, POOL_GROUP, POOL_GROUP), POOL_GROUP),
        "pool_scale": gain(ks[10], (L, D_POOL)),
        "gmlp_ln_g": gain(ks[11], (L, D_GMLP)),
        "gmlp_ln_b": 0.02 * jax.random.normal(ks[12], (L, D_GMLP), f32),
        "w_spatial": nrm(ks[13], (L, N_GMLP_HEADS, CHUNK, CHUNK), CHUNK),
        "b_spatial": gain(ks[14], (L, N_GMLP_HEADS, CHUNK)),
        "w_mix_out": nrm(ks[15], (L, D_MIX, D), D_MIX),
        "norm_ffn2_g": gain(ks[16], (L, D)),
        "ffn2_w_in": nrm(ks[17], (L, D, 2 * D_FF), D),
        "ffn2_w_out": nrm(ks[18], (L, D_FF, D), D_FF),
        "norm_final_g": gain(ks[19], (D,)),
    }

def reference(x, c, w_ada, b_ada, norm_ffn1_g, ffn1_w_in, ffn1_w_out,
              norm_mix_g, w_mix_in, w_pool, pool_scale, gmlp_ln_g, gmlp_ln_b,
              w_spatial, b_spatial, w_mix_out, norm_ffn2_g, ffn2_w_in, ffn2_w_out,
              norm_final_g):
    B = x.shape[0]
    c_act = jax.nn.silu(c)
    for l in range(DEPTH):
        mod = (c_act @ w_ada[l] + b_ada[l]).reshape(B, N_SUB, N_MOD, D_MODEL)

        h = modulate(rms_norm(x, norm_ffn1_g[l]), mod[:, 0, 0], mod[:, 0, 1])
        x = x + HALF_STEP * mod[:, 0, 2][:, None, :] * swiglu(h, ffn1_w_in[l], ffn1_w_out[l])

        h = modulate(rms_norm(x, norm_mix_g[l]), mod[:, 1, 0], mod[:, 1, 1])
        proj = h @ w_mix_in[l]
        xa = proj[..., :D_POOL]
        zb = proj[..., D_POOL:]
        ya = causal_multiscale_pool(xa, w_pool[l], pool_scale[l])
        yb = chunked_spatial_gating(zb, gmlp_ln_g[l], gmlp_ln_b[l], w_spatial[l], b_spatial[l])
        mix = jnp.concatenate([ya, yb], axis=-1) @ w_mix_out[l]
        x = x + mod[:, 1, 2][:, None, :] * mix

        h = modulate(rms_norm(x, norm_ffn2_g[l]), mod[:, 2, 0], mod[:, 2, 1])
        x = x + HALF_STEP * mod[:, 2, 2][:, None, :] * swiglu(h, ffn2_w_in[l], ffn2_w_out[l])
    return rms_norm(x, norm_final_g)


_drawn_inputs = setup_inputs


def setup_inputs(seed=0):
    import zlib

    import numpy as np

    out = dict(_drawn_inputs(seed))
    spreads = {}
    factors = {'norm_ffn1_g': 2.728,
     'pool_scale': 2.871,
     'gmlp_ln_g': 4.97,
     'gmlp_ln_b': 27.477,
     'b_spatial': 3.495,
     'norm_ffn2_g': 3.579}
    for name, (base, spread) in spreads.items():
        noise = np.random.default_rng([zlib.crc32(name.encode()), seed]).standard_normal(out[name].shape)
        drawn = base * np.exp(spread * noise) if base else spread * noise
        out[name] = __import__('jax').numpy.asarray(drawn.astype(out[name].dtype))
    for name, factor in factors.items():
        out[name] = (out[name] * factor).astype(out[name].dtype)
    return out
```

```python
from contextlib import ExitStack

import concourse.bass as bass
from concourse import mybir

P = 128
F32 = mybir.dt.float32
F32R = mybir.dt.float32r
ALU = mybir.AluOpType
ACT = mybir.ActivationFunctionType

EPS = 1e-6
HALF_STEP = 0.5
POOL_WINDOWS = (2, 4, 8, 16)
PAD = max(POOL_WINDOWS)


def build_program(nc, x, c, w_ada, b_ada, norm_ffn1_g, ffn1_w_in, ffn1_w_out, norm_mix_g, w_mix_in,
                  w_pool, pool_scale, gmlp_ln_g, gmlp_ln_b, w_spatial, b_spatial, w_mix_out,
                  norm_ffn2_g, ffn2_w_in, ffn2_w_out, norm_final_g, out):
    T, D = x.shape[1], x.shape[2]
    F = ffn1_w_out.shape[1]
    HEADS = w_spatial.shape[1]
    HC = D // 2 // HEADS
    KD, KF, KH = D // P, F // P, D // 2 // P
    NT = T // P
    NMOD = w_ada.shape[2] // P
    TILES = 2 * KD
    KC = KF // 2
    FULL, HALF = TILES * P, KC * P

    UP1 = 0
    DOWN1 = UP1 + KF
    MIXIN = DOWN1 + 2 * KD
    MIXOUT = MIXIN + 2 + KD // 2
    UP2 = MIXOUT + KD // 2
    DOWN2 = UP2 + KF
    END = DOWN2 + 2 * KD
    assert T == 512 and KF % 2 == 0 and D == 1024 and HEADS * HC == D // 2 and HC == 64

    FIRST = 2 * KD
    UNIT = 2 * P
    UNITS = (NMOD - FIRST) // 2
    assert KF < UNITS <= KF + KD and (UNITS - KF) % 2 == 0
    KA = KD // 2

    rows, at = {}, 0
    for name, n in (("b_ada", NMOD), ("g1", KD), ("gmix", KD), ("g2", KD), ("gfin", KD),
                    ("pool_scale", KH), ("c", KD)):
        rows[name] = at
        at += n
    NV = at

    ctx = ExitStack()
    with ctx:
        def sb(name, shape, dt=F32, scope=ctx):
            return scope.enter_context(nc.sbuf_tensor(name, shape, dt))

        def sem(name):
            return ctx.enter_context(nc.semaphore(name))

        xT = sb("xT", [P, KD, T])
        w_raw = sb("w_raw", [P, 2, FULL])
        w_hi = sb("w_hi", [P, 2, FULL], F32R)
        w_lo = sb("w_lo", [P, 2, FULL], F32R)
        ada_raw = sb("ada_raw", [P, 2, KA, UNIT])
        ada_acc = sb("ada_acc", [P, 2, UNIT])
        work = sb("work", [P, 3, T])
        wsT = sb("wsT", [P, HEADS, P])
        ident = sb("ident", [P, P])
        ones = sb("ones", [P, P])
        vcol = sb("vcol", [P, NV])
        c_act = sb("c_act", [P, KD])
        mod = sb("mod", [P, NMOD])
        gs = sb("gs", [P, 3, KD])
        half_gate = sb("half_gate", [P, 2, KD])
        small = sb("small", [P, 64])

        with ExitStack() as over_h:
            ws_raw = sb("ws_raw", [P, HEADS, P], F32, over_h)
            vrow = sb("vrow", [P, P], F32, over_h)
        with ExitStack() as over_h:
            out_tok = sb("out_tok", [P, NT, D], F32, over_h)
        h_hi = sb("h_hi", [P, KD, T], F32R)
        h_lo = sb("h_lo", [P, KD, T], F32R)
        with ExitStack() as over_a:
            ada_first = sb("ada_first", [P, KD, FIRST * P], F32, over_a)
            acc_first = sb("acc_first", [P, FIRST * P], F32, over_a)
            x_tok = sb("x_tok", [P, NT, D], F32, over_a)
        with ExitStack() as over_a:
            y_hi = sb("y_hi", [P, KD, T], F32R, over_a)
            y_lo = sb("y_lo", [P, KD, T], F32R, over_a)
            v_tok = sb("v_tok", [P, NT, KH * P], F32, over_a)
            xa = sb("xa", [P, KH, PAD + T], F32, over_a)
            pooled = sb("pooled", [P, KH, T], F32, over_a)
            u_gelu = sb("u_gelu", [P, KH, T], F32, over_a)
            window = sb("window", [P, 2, PAD + T], F32, over_a)
            ln_g = sb("ln_g", [P, KH * P], F32, over_a)
            ln_b = sb("ln_b", [P, KH * P], F32, over_a)
            bias_t = sb("bias_t", [P, KH, P], F32, over_a)
            wp = sb("wp", [P, KH, P], F32, over_a)
        a_hi = sb("a_hi", [P, KF, T], F32R)
        a_lo = sb("a_lo", [P, KF, T], F32R)

        ps = ctx.enter_context(nc.psum_tensor("ps", [P, 8, T], F32))
        SUM, MOD = 6, 7

        mv = small[:, 0:2 * NT].rearrange("p (t s) -> p t s", s=2)
        rstd_in = small[:, 8:8 + NT]
        rstd = small[:, 12:12 + NT]
        minus_half = small[:, 16:16 + NT]
        inv_count = small[:, 20:20 + PAD]
        r_out = small[:, 36:36 + NT]
        dummy = small[:, 40:41]
        eps_col = small[:, 41:42]
        stats = sb("stats", [P, NT, 6])

        raw_full = [sem("raw_full0"), sem("raw_full1")]
        hi_ready = sem("hi_ready")
        lo_ready = sem("lo_ready")
        chunk_done = sem("chunk_done")
        vec_full = sem("vec_full")
        x_full = sem("x_full")
        ws_full = sem("ws_full")
        first_full = [sem(f"first_full{k}") for k in range(KD)]
        ada_full = [sem("ada_full0"), sem("ada_full1")]
        mix_full = sem("mix_full")
        out_full = sem("out_full")
        consts = sem("consts")
        dve_const = sem("dve_const")
        ws_masked = sem("ws_masked")
        vec_T = sem("vec_T")
        vcol_ready = sem("vcol_ready")
        cact_ready = sem("cact_ready")
        first_step = sem("first_step")
        mod_done = sem("mod_done")
        mod_ready = sem("mod_ready")
        mod_link = sem("mod_link")
        x_T = sem("x_T")
        x_sq = sem("x_sq")
        ws_T = sem("ws_T")
        ws_ready = sem("ws_ready")
        sum_done = sem("sum_done")
        sq_summed = sem("sq_summed")
        root_ready = sem("root_ready")
        recip_ready = sem("recip_ready")
        scaled = sem("scaled")
        h_hi_ready = sem("h_hi_ready")
        h_ready = sem("h_ready")
        silu_ready = sem("silu_ready")
        prod_ready = sem("prod_ready")
        a_hi_ready = sem("a_hi_ready")
        a_ready = sem("a_ready")
        ada_link = sem("ada_link")
        ada_summed = sem("ada_summed")
        x_new = sem("x_new")
        sq_ready = sem("sq_ready")
        sq_added = sem("sq_added")
        v_gelu = sem("v_gelu")
        ln_stat = sem("ln_stat")
        ln_eps = sem("ln_eps")
        ln_rstd = sem("ln_rstd")
        ln_link = sem("ln_link")
        vn_ready = sem("vn_ready")
        pads = sem("pads")
        xa_ready = sem("xa_ready")
        win_link = sem("win_link")
        win_ready = sem("win_ready")
        pooled_link = sem("pooled_link")
        pooled_ready = sem("pooled_ready")
        mixed = sem("mixed")
        y_hi_ready = sem("y_hi_ready")
        y_ready = sem("y_ready")
        u_ready = sem("u_ready")
        spatial = sem("spatial")
        gate_link = sem("gate_link")
        y32_ready = sem("y32_ready")
        yg_scaled = sem("yg_scaled")
        out_T = sem("out_T")
        out_copied = sem("out_copied")
        r_ready = sem("r_ready")
        y_out = [sem("y_out_dve"), sem("y_out_act")]

        def up_w(w):
            return w[0].rearrange("(k p) (s n) -> p k s n", p=P, s=2)

        def down_w(w):
            return w[0].rearrange("(s k p) n -> p s k n", p=P, s=2)

        def kpn(w):
            return w[0].rearrange("(k p) n -> p k n", p=P)

        w_ada_v = kpn(w_ada)

        def pair_view(ring, s):
            return ring[:, s].rearrange("p (s k n) -> p s k n", s=2, n=P)

        def half_view(ring, s):
            return ring[:, s, 0:HALF].rearrange("p (k n) -> p k n", n=P)

        def v_view(ring, s):
            return ring[:, s].rearrange("p (k n) -> p k n", n=KH * P)

        def mod_col(section, k):
            return mod[:, section * KD + k:section * KD + k + 1]

        def vec(name, k):
            return vcol[:, rows[name] + k:rows[name] + k + 1]

        block = ctx.enter_context(nc.Block())

        @block.sync
        def _(sp):
            def raw_free(chunk):
                if not (isinstance(chunk, int) and chunk < 2):
                    sp.wait_ge(lo_ready, chunk - 1)

            def load_pair(w, j, s, chunk):
                raw_free(chunk)
                for g in range(2):
                    sp.dma_start(pair_view(w_raw, s)[:, g], up_w(w)[:, :, g, bass.ds(j * P, P)])\
                      .then_inc(raw_full[s], 16)

            def load_two(w, col, s, chunk):
                raw_free(chunk)
                for g in range(2):
                    sp.dma_start(pair_view(w_raw, s)[:, g], kpn(w)[:, :, col + g * P:col + (g + 1) * P])\
                      .then_inc(raw_full[s], 16)

            def load_v(w, kq, s, chunk):
                raw_free(chunk)
                for g in range(2):
                    k0 = kq * 4 + 2 * g
                    sp.dma_start(v_view(w_raw, s)[:, 2 * g:2 * g + 2],
                                 kpn(w)[:, k0:k0 + 2, 2 * KH * P:3 * KH * P]).then_inc(raw_full[s], 16)

            def load_down(w, m, s, chunk):
                raw_free(chunk)
                for g, (k0, k1) in enumerate(((0, KC // 2), (KC // 2, KC))):
                    sp.dma_start(half_view(w_raw, s)[:, k0:k1], down_w(w)[:, s, k0:k1, bass.ds(m * P, P)])\
                      .then_inc(raw_full[s], 16)

            def load_ada(u):
                for s in range(2):
                    if not (isinstance(u, int) and u == 0):
                        sp.wait_ge(ada_link, u * KD - KA * (1 - s))
                    sp.dma_start(ada_raw[:, s], w_ada_v[:, s * KA:(s + 1) * KA,
                                                        bass.ds(u * UNIT + FIRST * P, UNIT)])\
                      .then_inc(ada_full[s], 16)

            def load_vec(name, v):
                n = v.shape[-1] // P
                sp.dma_start(vrow[rows[name]:rows[name] + n, :], v.rearrange("a (k p) -> (a k) p", p=P))\
                  .then_inc(vec_full, 16)

            def load_first(k):
                sp.dma_start(ada_first[:, k, :], w_ada_v[:, k, 0:FIRST * P]).then_inc(first_full[k], 16)

            load_vec("c", c)
            load_vec("b_ada", b_ada)
            load_first(0)
            for name, v in (("g1", norm_ffn1_g), ("gmix", norm_mix_g), ("g2", norm_ffn2_g),
                            ("gfin", norm_final_g.rearrange("(a d) -> a d", a=1)),
                            ("pool_scale", pool_scale)):
                load_vec(name, v)
            for t in range(NT):
                sp.dma_start(x_tok[:, t, :], x[0, t * P:(t + 1) * P, :]).then_inc(x_full, 16)
            for k in range(1, KD - 2):
                load_first(k)
            sp.dma_start(ws_raw[:], w_spatial[0].rearrange("h t s -> t h s")).then_inc(ws_full, 16)
            load_pair(ffn1_w_in, 0, 0, 0)
            load_first(KD - 2)
            load_first(KD - 1)
            load_pair(ffn1_w_in, 1, 1, 1)
            load_ada(0)
            load_ada(1)

            with sp.Fori(1, KF // 2) as i:
                for s in range(2):
                    load_pair(ffn1_w_in, i * 2 + s, s, i * 2 + s + UP1)
                    load_ada(i * 2 + s)

            with sp.Fori(0, (UNITS - KF) // 2) as i:
                for q in range(2):
                    for s in range(2):
                        load_down(ffn1_w_out, i * 2 + q, s, i * 4 + 2 * q + s + DOWN1)
                    load_ada(i * 2 + q + KF)
            for m in range(UNITS - KF, KD):
                for s in range(2):
                    load_down(ffn1_w_out, m, s, DOWN1 + 2 * m + s)

            for s in range(2):
                load_v(w_mix_in, s, s, MIXIN + s)
            for q in range(2):
                load_two(w_mix_in, q * UNIT, q, MIXIN + 2 + q)
            sp.wait_ge(chunk_done, MIXIN)
            sp.dma_start(wp[:], w_pool[0].rearrange("g c d -> c g d")).then_inc(mix_full, 16)
            sp.dma_start(ln_g[:], gmlp_ln_g.to_broadcast([P, KH * P])).then_inc(mix_full, 16)
            sp.dma_start(ln_b[:], gmlp_ln_b.to_broadcast([P, KH * P])).then_inc(mix_full, 16)
            for h in range(HEADS):
                sp.dma_start(bias_t[(h % 2) * HC:(h % 2 + 1) * HC, h // 2, :],
                             b_spatial[0, h:h + 1, :].to_broadcast([HC, P])).then_inc(mix_full, 16)
            for q in range(2, 4):
                load_two(w_mix_in, q * UNIT, q % 2, MIXIN + 2 + q)
            for q in range(KD // 2):
                load_two(w_mix_out, q * UNIT, q % 2, MIXOUT + q)

            with sp.Fori(0, KF // 2) as i:
                for s in range(2):
                    load_pair(ffn2_w_in, i * 2 + s, s, i * 2 + s + UP2)
            with sp.Fori(0, KD) as m:
                for s in range(2):
                    load_down(ffn2_w_out, m, s, m * 2 + s + DOWN2)

            for t in range(NT):
                sp.wait_ge(y_out[t % 2], t // 2 + 1)
                sp.dma_start(out[0, t * P:(t + 1) * P, :], out_tok[:, t, :]).then_inc(out_full, 16)
            sp.wait_ge(out_full, 16 * NT)

        @block.gpsimd
        def _(pool):
            nc.gpsimd.memset(ident[:], 0.0).then_inc(consts, 1)
            pool.wait_ge(consts, 1)
            nc.gpsimd.affine_select(out=ident[:], in_=ident[:], compare_op=ALU.not_equal, fill=1.0,
                                    base=0, pattern=[[-1, P]], channel_multiplier=1).then_inc(consts, 1)
            nc.gpsimd.memset(minus_half, -0.5).then_inc(consts, 1)
            pool.wait_ge(ws_full, 16)
            nc.gpsimd.affine_select(out=ws_raw[:], in_=ws_raw[:], compare_op=ALU.is_ge, fill=0.0,
                                    base=0, pattern=[[0, HEADS], [-1, P]], channel_multiplier=1)\
                .then_inc(ws_masked, 1)

            pool.wait_ge(chunk_done, MIXIN)
            nc.gpsimd.memset(xa[:, :, 0:PAD], 0.0).then_inc(pads, 1)
            nc.gpsimd.memset(window[:, :, 0:PAD], 0.0).then_inc(pads, 1)
            pool.wait_ge(ln_stat, NT)
            nc.gpsimd.tensor_scalar(rstd_in, mv[:, :, 1], EPS, 0.0, ALU.add, ALU.add).then_inc(ln_eps, 1)
            pool.wait_ge(ln_eps, 1)
            pool.wait_ge(consts, 3)
            nc.gpsimd.tensor_tensor(rstd, rstd_in, minus_half, ALU.pow).then_inc(ln_rstd, 1)
            link = 0
            for g, w in enumerate(POOL_WINDOWS):
                pool.wait_ge(xa_ready, g + 1)
                if g == 0:
                    pool.wait_ge(pads, 2)
                src, d, n = xa[:, g], 1, 0
                while d < w:
                    if g and n == 0:
                        pool.wait_ge(pooled_ready, g)
                    dst = window[:, n % 2]
                    ins = nc.gpsimd.tensor_tensor(dst[:, PAD:PAD + T], src[:, PAD:PAD + T],
                                                  src[:, PAD - d:PAD - d + T], ALU.add)
                    d *= 2
                    n += 1
                    src = dst
                    if d < w:
                        ins.then_inc(win_link, 1)
                        link += 1
                        pool.wait_ge(win_link, link)
                    else:
                        ins.then_inc(win_ready, 1)

        @block.scalar
        def _(act):
            def split_hi(s, n, chunk):
                number, half = (chunk, chunk // 2) if isinstance(chunk, int) else chunk
                act.wait_ge(raw_full[s], half * 32 + 32)
                if not (isinstance(number, int) and number < 2):
                    act.wait_ge(chunk_done, number - 1)
                nc.scalar.copy(w_hi[:, s, 0:n], w_raw[:, s, 0:n]).then_inc(hi_ready, 1)

            def h_his(count0, shift_section):
                for k in range(KD):
                    act.wait_ge(scaled, count0 + k + 1)
                    nc.scalar.activation(h_hi[:, k, :], work[:, k % 2, :], ACT.Identity,
                                         bias=mod_col(shift_section, k)).then_inc(h_hi_ready, 1)

            def root(n):
                act.wait_ge(sum_done, n)
                nc.scalar.activation(work[:, 2, :], ps[:, SUM, :], ACT.Sqrt, bias=eps_col,
                                     scale=1.0 / D).then_inc(root_ready, 1)

            act.wait_ge(dve_const, 2)
            act.wait_ge(vcol_ready, 1)
            nc.scalar.activation(c_act[:], vcol[:, rows["c"]:rows["c"] + KD], ACT.Silu).then_inc(cact_ready, 1)
            for k in range(KD):
                act.wait_ge(x_T, k + 1)
                nc.scalar.copy(xT[:, k, :], ps[:, k % 4, :])
                if k >= 2:
                    act.wait_ge(sq_summed, k - 1)
                nc.scalar.activation(work[:, k % 2, :], ps[:, k % 4, :], ACT.Square).then_inc(x_sq, 1)
            root(1)
            for q in range(2):
                act.wait_ge(ws_T, q + 1)
                nc.scalar.copy(wsT[:, 4 * q:4 * q + 4, :],
                               ps[:, 4 + q, :].rearrange("p (h t) -> p h t", h=4)).then_inc(ws_ready, 1)
            split_hi(0, FULL, 0)
            act.wait_ge(mod_ready, 1)
            h_his(0, 0)
            split_hi(1, FULL, 1)

            def up_step(j, jn, s, n_next, nxt):
                act.wait_ge(chunk_done, nxt[0] - 1)
                if not (isinstance(jn, int) and jn == 0):
                    act.wait_ge(prod_ready, jn)
                nc.scalar.activation(work[:, 0, :], ps[:, 2 * s, :], ACT.Silu).then_inc(silu_ready, 1)
                split_hi(s, n_next, nxt)
                act.wait_ge(prod_ready, jn + 1)
                nc.scalar.copy(a_hi[:, bass.ds(j, 1), :], work[:, 1:2, :]).then_inc(a_hi_ready, 1)

            def up(base, nth):
                for j in range(2):
                    up_step(j, j + nth * KF, j, FULL, (base + j + 2, base // 2 + 1))
                with act.Fori(1, KF // 2 - 1) as i:
                    for s in range(2):
                        up_step(i * 2 + s, i * 2 + (s + nth * KF), s, FULL,
                                (i * 2 + (s + base + 2), i + (base // 2 + 1)))
                for s in range(2):
                    j = KF - 2 + s
                    up_step(j, j + nth * KF, s, HALF, (base + j + 2, (base + j + 2) // 2))

            def square(m, x_count, added):
                act.wait_ge(x_new, x_count + 1)
                act.wait_ge(sq_added, added)
                src = xT[:, m, :] if isinstance(m, int) else xT[:, bass.ds(m, 1), :]
                dst = work[:, 0, :] if isinstance(m, int) else work[:, 0:1, :]
                nc.scalar.activation(dst, src, ACT.Square).then_inc(sq_ready, 1)

            def copy_out(m):
                act.wait_ge(out_T, m + 1)
                src = ps[:, SUM, :].rearrange("p (t f) -> p t f", t=NT)
                nc.scalar.copy(out_tok[:, :, bass.ds(m * P, P)], src).then_inc(out_copied, 1)

            def down(base, x_count, sq_count, last):
                nc.scalar.activation(dummy, ones[:, 0:1], ACT.Sqrt)
                with act.Fori(0, KD - 1) as m:
                    for s in range(2):
                        split_hi(s, HALF, (m * 2 + (base + s + 2), m + (base // 2 + 1)))
                    square(m, m + x_count, m + (sq_count + 1))
                    if last:
                        copy_out(m)
                if not last:
                    for s in range(2):
                        split_hi(s, FULL, base + 2 * KD + s)
                square(KD - 1, x_count + KD - 1, sq_count + KD)
                if last:
                    copy_out(KD - 1)

            up(UP1, 0)
            down(DOWN1, 0, 0, False)
            root(2)
            h_his(KD, 3)

            split_hi(0, FULL, MIXIN + 2)
            split_hi(1, FULL, MIXIN + 3)
            for t in range(NT):
                act.wait_ge(chunk_done, MIXIN + 2)
                nc.scalar.activation(v_tok[:, t, :], ps[:, t, :], ACT.Gelu_apprx_tanh).then_inc(v_gelu, 1)
            for q in range(2):
                act.wait_ge(chunk_done, MIXIN + 3 + q)
                for g in range(2):
                    nc.scalar.copy(xa[:, 2 * q + g, PAD:PAD + T], ps[:, (4, 5, 0, 1)[2 * q + g], :])\
                        .then_inc(xa_ready, 1)
                split_hi(q, FULL, MIXIN + 4 + q)
            for q in range(2):
                act.wait_ge(chunk_done, MIXIN + 5 + q)
                for g in range(2):
                    nc.scalar.activation(u_gelu[:, 2 * q + g, :], ps[:, (2, 3, 4, 5)[2 * q + g], :],
                                         ACT.Gelu_apprx_tanh).then_inc(u_ready, 1)
                if q == 0:
                    split_hi(0, FULL, MIXOUT)
            for g in range(KH):
                act.wait_ge(mixed, g + 1)
                nc.scalar.activation(y_hi[:, g, :], ps[:, (6, 7, 0, 1)[g], :], ACT.Identity,
                                     scale=vec("pool_scale", g)).then_inc(y_hi_ready, 1)
            split_hi(1, FULL, MIXOUT + 1)
            for g in range(KH):
                act.wait_ge(y32_ready, g + 1)
                nc.scalar.copy(y_hi[:, KH + g, :], pooled[:, g, :]).then_inc(y_hi_ready, 1)
            nc.scalar.activation(dummy, ones[:, 0:1], ACT.Sqrt)
            for q in range(KD // 2):
                split_hi(q % 2, FULL, MIXOUT + 2 + q)
                for g in range(2):
                    m = 2 * q + g
                    square(m, KD + m, KD + m + 1)
            root(3)
            h_his(2 * KD, 6)

            up(UP2, 1)
            down(DOWN2, 2 * KD, 2 * KD, True)
            act.wait_ge(sum_done, 4)
            nc.scalar.activation(r_out, ps[:, MOD, 0:NT], ACT.Sqrt, bias=eps_col, scale=1.0 / D)\
                .then_inc(root_ready, 1)
            act.wait_ge(r_ready, 1)
            act.wait_ge(out_copied, KD)
            for t in range(1, NT, 2):
                nc.scalar.activation(out_tok[:, t, :], out_tok[:, t, :], ACT.Copy,
                                     scale=r_out[:, t:t + 1]).then_inc(y_out[1], 1)

        @block.vector
        def _(dve):
            def split_lo(s, n, number):
                dve.wait_ge(hi_ready, number + 1)
                nc.vector.tensor_tensor(w_lo[:, s, 0:n], w_raw[:, s, 0:n], w_hi[:, s, 0:n].bitcast(F32),
                                        ALU.subtract).then_inc(lo_ready, 1)

            def norm(n, count0, shift_section):
                dve.wait_ge(root_ready, n + 1)
                nc.vector.reciprocal(work[:, 2, :], work[:, 2, :]).then_inc(recip_ready, 1)
                dve.wait_ge(recip_ready, n + 1)

                def lo(k):
                    dve.wait_ge(h_hi_ready, count0 + k + 1)
                    nc.vector.scalar_tensor_tensor(
                        h_lo[:, k, :], work[:, k % 2, :], mod_col(shift_section, k),
                        h_hi[:, k, :].bitcast(F32), ALU.add, ALU.subtract).then_inc(h_ready, 1)

                for k in range(KD):
                    if k >= 2:
                        dve.wait_ge(h_ready, count0 + k - 1)
                    nc.vector.scalar_tensor_tensor(work[:, k % 2, :], xT[:, k, :], gs[:, n, k:k + 1],
                                                   work[:, 2, :], ALU.mult, ALU.mult).then_inc(scaled, 1)
                    if k >= 1:
                        lo(k - 1)
                lo(KD - 1)

            def gains(n, name, scale_section):
                nc.vector.scalar_tensor_tensor(
                    gs[:, n, :], mod[:, scale_section * KD:(scale_section + 1) * KD], 1.0,
                    vcol[:, rows[name]:rows[name] + KD], ALU.add, ALU.mult).then_inc(mod_ready, 1)

            def take_mod(c0, c1, n):
                nc.vector.tensor_tensor(mod[:, c0:c1], ps[:, MOD, c0:c1],
                                        vcol[:, rows["b_ada"] + c0:rows["b_ada"] + c1], ALU.add)\
                    .then_inc(mod_link, 1)
                dve.wait_ge(mod_link, n)

            def ada_unit(u, s_acc):
                if not (isinstance(u, int) and u < 2):
                    dve.wait_ge(ada_summed, u - 1)
                for k in range(KD):
                    if k % KA == 0:
                        dve.wait_ge(ada_full[k // KA], u * 16 + 16)
                    w = ada_raw[:, k // KA, k % KA, :]
                    if k == 0:
                        ins = nc.vector.tensor_scalar(ada_acc[:, s_acc, :], w, c_act[:, 0:1], None, ALU.mult)
                    else:
                        dve.wait_ge(ada_link, u * KD + k)
                        ins = nc.vector.scalar_tensor_tensor(ada_acc[:, s_acc, :], w, c_act[:, k:k + 1],
                                                             ada_acc[:, s_acc, :], ALU.mult, ALU.add)
                    ins.then_inc(ada_link, 1)

            def up_step(j, jn, s, base, n_next, ada):
                if ada:
                    ada_unit(j, s)
                dve.wait_ge(silu_ready, jn + 1)
                if not (isinstance(jn, int) and jn == 0):
                    dve.wait_ge(a_ready, jn)
                nc.vector.tensor_tensor(work[:, 1, :], work[:, 0, :], ps[:, 2 * s + 1, :], ALU.mult)\
                    .then_inc(prod_ready, 1)
                split_lo(s, n_next, j + (base + 2))
                dve.wait_ge(a_hi_ready, jn + 1)
                if isinstance(j, int):
                    dst, prod, hi = a_lo[:, j, :], work[:, 1, :], a_hi[:, j, :]
                else:
                    dst, prod, hi = a_lo[:, bass.ds(j, 1), :], work[:, 1:2, :], a_hi[:, bass.ds(j, 1), :]
                nc.vector.tensor_tensor(dst, prod, hi.bitcast(F32), ALU.subtract).then_inc(a_ready, 1)

            def up(base, nth, ada):
                if ada:
                    for s in range(2):
                        up_step(s, s, s, base, FULL, ada)
                with dve.Fori(1 if ada else 0, KF // 2 - 1) as i:
                    for s in range(2):
                        up_step(i * 2 + s, i * 2 + (s + nth * KF), s, base, FULL, ada)
                for s in range(2):
                    j = KF - 2 + s
                    up_step(j, j + nth * KF, s, base, HALF, ada)

            def update(m, n_mm, bank, gate, x_dst):
                dve.wait_ge(chunk_done, n_mm)
                nc.vector.scalar_tensor_tensor(x_dst, ps[:, bank:bank + 1, :], gate, x_dst,
                                               ALU.mult, ALU.add).then_inc(x_new, 1)

            def add_squares(sq_n):
                dve.wait_ge(sq_ready, sq_n)
                nc.vector.tensor_tensor(work[:, 1, :], work[:, 1, :], work[:, 0, :], ALU.add)\
                    .then_inc(sq_added, 1)

            def final_gain(m, x_count):
                dve.wait_ge(x_new, x_count + 1)
                if not (isinstance(m, int) and m == 0):
                    dve.wait_ge(out_T, m)
                if isinstance(m, int):
                    src, g = xT[:, m, :], vec("gfin", m)
                else:
                    src, g = xT[:, bass.ds(m, 1), :], vcol[:, bass.ds(m + rows["gfin"], 1)]
                dst = work[:, 2, :] if isinstance(m, int) else work[:, 2:3, :]
                nc.vector.tensor_scalar(dst, src, g, None, ALU.mult).then_inc(yg_scaled, 1)

            def down(base, x_count, sq_count, gate_n, ada, last):
                dve.wait_ge(a_ready, (gate_n + 1) * KF)
                nc.vector.memset(work[:, 1, :], 0.0).then_inc(sq_added, 1)

                def step(m, units):
                    q = m if isinstance(m, int) else None
                    for s in range(2):
                        if q != KD - 1 or not last:
                            split_lo(s, FULL if q == KD - 1 else HALF, m * 2 + (base + 2 + s))
                    if units is not None:
                        ada_unit(*units)
                    gate = half_gate[:, gate_n, m:m + 1] if q is not None \
                        else half_gate[:, gate_n, bass.ds(m, 1)]
                    return gate

                def block_of(m, bank, units):
                    gate = step(m, units)
                    x_dst = xT[:, m:m + 1, :] if isinstance(m, int) else xT[:, bass.ds(m, 1), :]
                    update(m, m * 2 + (base + 2), bank, gate, x_dst)
                    if last:
                        final_gain(m, m + x_count)
                    if not (isinstance(m, int) and m == KD - 1):
                        add_squares(m + (sq_count + 1))

                pairs = (UNITS - KF) // 2 if ada else KD // 2 - 1
                if last:
                    for q in range(2):
                        block_of(q, 4 + q, None)
                with dve.Fori(1 if last else 0, pairs) as i:
                    for q in range(2):
                        block_of(i * 2 + q, 4 + q, (i * 2 + (q + KF), q) if ada else None)
                for m in range(2 * pairs, KD):
                    block_of(m, 4 + m % 2, None)

            nc.vector.memset(ones[:], 1.0).then_inc(dve_const, 1)
            nc.vector.memset(eps_col, EPS).then_inc(dve_const, 1)
            for t in range(PAD):
                nc.vector.memset(inv_count[:, t:t + 1], 1.0 / (t + 1)).then_inc(dve_const, 1)
            dve.wait_ge(dve_const, 2 + PAD)
            dve.wait_ge(vec_T, 1)
            nc.vector.tensor_copy(vcol[:], ps[:, SUM, 0:NV]).then_inc(vcol_ready, 1)
            dve.wait_ge(cact_ready, 1)
            for k in range(KD):
                dve.wait_ge(first_full[k], 16)
                w = ada_first[:, k, :]
                if k == 0:
                    ins = nc.vector.tensor_scalar(acc_first[:], w, c_act[:, 0:1], None, ALU.mult)
                else:
                    dve.wait_ge(first_step, k)
                    ins = nc.vector.scalar_tensor_tensor(acc_first[:], w, c_act[:, k:k + 1], acc_first[:],
                                                         ALU.mult, ALU.add)
                ins.then_inc(first_step, 1)
            split_lo(0, FULL, 0)
            dve.wait_ge(mod_done, 1)
            take_mod(0, FIRST, 1)
            gains(0, "g1", 1)
            dve.wait_ge(mod_ready, 1)
            norm(0, 0, 0)
            split_lo(1, FULL, 1)

            up(UP1, 0, True)
            dve.wait_ge(ada_summed, KF)
            take_mod(FIRST, FIRST + 2 * KF, 2)
            nc.vector.tensor_scalar(half_gate[:, 0, :], mod[:, 2 * KD:3 * KD], HALF_STEP, None, ALU.mult)\
                .then_inc(mod_ready, 1)
            dve.wait_ge(mod_ready, 2)
            down(DOWN1, 0, 0, 0, True, False)
            dve.wait_ge(ada_summed, UNITS)
            take_mod(FIRST + 2 * KF, NMOD, 3)
            gains(1, "gmix", 4)
            gains(2, "g2", 7)
            nc.vector.tensor_scalar(half_gate[:, 1, :], mod[:, 8 * KD:9 * KD], HALF_STEP, None, ALU.mult)\
                .then_inc(mod_ready, 1)
            dve.wait_ge(mod_ready, 5)
            norm(1, KD, 3)

            for s in range(2):
                split_lo(s, FULL, MIXIN + 2 + s)
            for t in range(NT):
                dve.wait_ge(v_gelu, t + 1)
                nc.vector.bn_stats(stats[:, t, :], v_tok[:, t, :]).then_inc(ln_link, 1)
            for t in range(NT):
                dve.wait_ge(ln_link, t + 1)
                nc.vector.bn_aggr(mv[:, t, :], stats[:, t, :]).then_inc(ln_stat, 1)
            dve.wait_ge(ln_rstd, 1)
            for t in range(NT):
                nc.vector.tensor_scalar(v_tok[:, t, :], v_tok[:, t, :], mv[:, t, 0:1], rstd[:, t:t + 1],
                                        ALU.subtract, ALU.mult).then_inc(ln_link, 1)
            dve.wait_ge(mix_full, 16 * (3 + HEADS))
            for t in range(NT):
                dve.wait_ge(ln_link, NT + t + 1)
                nc.vector.tensor_tensor(v_tok[:, t, :], v_tok[:, t, :], ln_g[:], ALU.mult).then_inc(ln_link, 1)
            for t in range(NT):
                dve.wait_ge(ln_link, 2 * NT + t + 1)
                nc.vector.tensor_tensor(v_tok[:, t, :], v_tok[:, t, :], ln_b[:], ALU.add).then_inc(vn_ready, 1)
            split_lo(0, FULL, MIXIN + 4)
            for g, w in enumerate(POOL_WINDOWS):
                if g == 2:
                    split_lo(1, FULL, MIXIN + 5)
                dve.wait_ge(win_ready, g + 1)
                wsum = window[:, (w.bit_length() - 2) % 2]
                nc.vector.tensor_tensor(pooled[:, g, 0:w], wsum[:, PAD:PAD + w], inv_count[:, 0:w], ALU.mult)\
                    .then_inc(pooled_link, 1)
                nc.vector.scalar_tensor_tensor(pooled[:, g, w:T], wsum[:, PAD + w:PAD + T], 1.0 / w,
                                               xa[:, g, PAD + w:PAD + T], ALU.mult, ALU.subtract)\
                    .then_inc(pooled_link, 1)
                dve.wait_ge(pooled_link, 2 * g + 2)
                nc.vector.tensor_tensor(pooled[:, g, 0:w], pooled[:, g, 0:w], xa[:, g, PAD:PAD + w],
                                        ALU.subtract).then_inc(pooled_ready, 1)
            split_lo(0, FULL, MIXOUT)
            for g in range(KH):
                dve.wait_ge(y_hi_ready, g + 1)
                nc.vector.scalar_tensor_tensor(y_lo[:, g, :], ps[:, (6, 7, 0, 1)[g], :], vec("pool_scale", g),
                                               y_hi[:, g, :].bitcast(F32), ALU.mult, ALU.subtract)\
                    .then_inc(y_ready, 1)
            split_lo(1, FULL, MIXOUT + 1)
            for g in range(KH):
                dve.wait_ge(spatial, g + 1)
                dve.wait_ge(u_ready, g + 1)
                v3 = pooled[:, g, :].rearrange("p (n t) -> p n t", n=NT)
                sv3 = ps[:, (2, 3, 6, 7)[g], :].rearrange("p (n t) -> p n t", n=NT)
                b3 = bias_t[:, g:g + 1, :].to_broadcast([P, NT, P])
                nc.vector.tensor_tensor(v3, sv3, b3, ALU.add).then_inc(gate_link, 1)
                dve.wait_ge(gate_link, g + 1)
                nc.vector.tensor_tensor(pooled[:, g, :], pooled[:, g, :], u_gelu[:, g, :], ALU.mult)\
                    .then_inc(y32_ready, 1)
                if g:
                    dve.wait_ge(y_hi_ready, KH + g)
                    nc.vector.tensor_tensor(y_lo[:, KH + g - 1, :], pooled[:, g - 1, :],
                                            y_hi[:, KH + g - 1, :].bitcast(F32), ALU.subtract)\
                        .then_inc(y_ready, 1)
            dve.wait_ge(y_hi_ready, 2 * KH)
            nc.vector.tensor_tensor(y_lo[:, KD - 1, :], pooled[:, KH - 1, :],
                                    y_hi[:, KD - 1, :].bitcast(F32), ALU.subtract).then_inc(y_ready, 1)
            nc.vector.memset(work[:, 1, :], 0.0).then_inc(sq_added, 1)
            for q in range(KD // 2):
                split_lo(q % 2, FULL, MIXOUT + 2 + q)
                for g in range(2):
                    m = 2 * q + g
                    update(m, MIXOUT + q + 1, 2 * (q % 2) + g, mod_col(5, m), xT[:, m:m + 1, :])
                    if m < KD - 1:
                        add_squares(KD + m + 1)
            norm(2, 2 * KD, 6)

            up(UP2, 1, False)
            down(DOWN2, 2 * KD, 2 * KD, 1, False, True)
            dve.wait_ge(root_ready, 4)
            nc.vector.reciprocal(r_out, r_out).then_inc(r_ready, 1)
            dve.wait_ge(r_ready, 1)
            dve.wait_ge(out_copied, KD)
            for t in range(0, NT, 2):
                nc.vector.tensor_scalar(out_tok[:, t, :], out_tok[:, t, :], r_out[:, t:t + 1], None, ALU.mult)\
                    .then_inc(y_out[0], 1)

        @block.tensor
        def _(pe):
            def product(dst, w_h, w_l, a_h, a_l, start, stop):
                nc.tensor.matmul(dst, w_h, a_h, start=start, stop=False)
                nc.tensor.matmul(dst, w_l, a_h, start=False, stop=False)
                return nc.tensor.matmul(dst, w_h, a_l, start=False, stop=stop)

            def pair(s, number, banks, src_hi, src_lo, wait_k=None):
                pe.wait_ge(lo_ready, number + 1)
                hi, lo = pair_view(w_hi, s), pair_view(w_lo, s)
                for k in range(KD):
                    if wait_k:
                        wait_k(k)
                    for g in range(2):
                        ins = product(ps[:, banks[g], :], hi[:, g, k, :], lo[:, g, k, :],
                                      src_hi[:, k, :], src_lo[:, k, :], k == 0, k == KD - 1)
                ins.then_inc(chunk_done, 1)

            def sum_unit(u, s):
                pe.wait_ge(ada_link, u * KD + KD)
                for t in range(2):
                    if isinstance(u, int):
                        col = FIRST + 2 * u + t
                        dst = ps[:, MOD, col:col + 1]
                    else:
                        dst = ps[:, MOD, bass.ds(u * 2 + (FIRST + t), 1)]
                    ins = nc.tensor.matmul(dst, ada_acc[:, s, t * P:(t + 1) * P], ones[:, 0:1],
                                           start=True, stop=True)
                ins.then_inc(ada_summed, 1)

            def up(base, nth, ada):
                def h_block(k):
                    pe.wait_ge(h_ready, (2 * nth) * KD + k + 1)

                def step(j, s, wait_k=None):
                    if not (isinstance(j, int) and j < 2):
                        pe.wait_ge(prod_ready, j + (nth * KF - 1))
                    pair(s, j + base, (2 * s, 2 * s + 1), h_hi, h_lo, wait_k)
                    if ada:
                        sum_unit(j, s)

                step(0, 0, h_block)
                step(1, 1)
                with pe.Fori(1, KF // 2) as i:
                    for s in range(2):
                        step(i * 2 + s, s)

            def down(base, gate_n, x_count, ada, last):
                def block_of(m, bank, u):
                    if not (isinstance(m, int) and m < 2):
                        pe.wait_ge(x_new, m + (x_count - 1))
                    for s in range(2):
                        pe.wait_ge(lo_ready, m * 2 + (base + s + 1))
                        pe.wait_ge(a_ready, gate_n * KF + (KC if s == 0 else KF))
                        hi, lo = half_view(w_hi, s), half_view(w_lo, s)
                        for k in range(KC):
                            ins = product(ps[:, bank, :], hi[:, k, :], lo[:, k, :],
                                          a_hi[:, s * KC + k, :], a_lo[:, s * KC + k, :],
                                          s == 0 and k == 0, s == 1 and k == KC - 1)
                        ins.then_inc(chunk_done, 1)
                        if last and s == 0 and not (isinstance(m, int) and m == 0):
                            transpose_out(m - 1)
                    if u is not None:
                        sum_unit(*u)

                pairs = (UNITS - KF) // 2 if ada else KD // 2
                if ada:
                    pe.wait_ge(mod_ready, 2)
                for m in range(2):
                    block_of(m, 4 + m, (KF + m, m) if ada else None)
                with pe.Fori(1, pairs) as i:
                    for q in range(2):
                        block_of(i * 2 + q, 4 + q, (i * 2 + (KF + q), q) if ada else None)
                for m in range(2 * pairs, KD):
                    block_of(m, 4 + m % 2, None)

            def transpose_out(m):
                pe.wait_ge(yg_scaled, m + 1)
                if not (isinstance(m, int) and m == 0):
                    pe.wait_ge(out_copied, m)
                for t in range(NT):
                    ins = nc.tensor.transpose(ps[:, SUM, t * P:(t + 1) * P], work[:, 2, t * P:(t + 1) * P],
                                              ident[:])
                ins.then_inc(out_T, 1)

            def sum_squares(sq_n):
                pe.wait_ge(sq_added, sq_n)
                nc.tensor.matmul(ps[:, SUM, :], ones[:], work[:, 1, :], start=True, stop=False)
                pe.wait_ge(sq_ready, sq_n)
                nc.tensor.matmul(ps[:, SUM, :], ones[:], work[:, 0, :], start=False, stop=True)\
                    .then_inc(sum_done, 1)

            pe.wait_ge(consts, 2)
            pe.wait_ge(vec_full, 16 * len(rows))
            nc.tensor.transpose(ps[:, SUM, 0:NV], vrow[0:NV, :], ident[0:NV, 0:NV]).then_inc(vec_T, 1)
            pe.wait_ge(x_full, 16 * NT)
            pe.wait_ge(dve_const, 1)
            pe.wait_ge(vcol_ready, 1)

            def sum_x(k):
                pe.wait_ge(x_sq, k + 1)
                ins = nc.tensor.matmul(ps[:, SUM, :], ones[:], work[:, k % 2, :], start=k == 0,
                                       stop=k == KD - 1)
                ins.then_inc(sq_summed if k < KD - 1 else sum_done, 1)

            for k in range(KD):
                if k >= 4:
                    pe.wait_ge(x_sq, k - 3)
                for t in range(NT):
                    ins = nc.tensor.transpose(ps[:, k % 4, t * P:(t + 1) * P],
                                              x_tok[:, t, k * P:(k + 1) * P], ident[:])
                ins.then_inc(x_T, 1)
                if k >= 1:
                    sum_x(k - 1)
            sum_x(KD - 1)
            pe.wait_ge(ws_masked, 1)
            for q in range(2):
                for h in range(4):
                    ins = nc.tensor.transpose(ps[:, 4 + q, h * P:(h + 1) * P], ws_raw[:, 4 * q + h, :], ident[:])
                ins.then_inc(ws_T, 1)
            pe.wait_ge(first_step, KD)
            for col in range(FIRST):
                ins = nc.tensor.matmul(ps[:, MOD, col:col + 1], acc_first[:, col * P:(col + 1) * P],
                                       ones[:, 0:1], start=True, stop=True)
            ins.then_inc(mod_done, 1)
            pe.wait_ge(mod_ready, 1)

            up(UP1, 0, True)
            down(DOWN1, 0, 0, True, False)
            sum_squares(KD)

            for s in range(2):
                pe.wait_ge(lo_ready, MIXIN + s + 1)
                hi, lo = v_view(w_hi, s), v_view(w_lo, s)
                for k in range(4):
                    pe.wait_ge(h_ready, KD + 4 * s + k + 1)
                    for t in range(NT):
                        ks, ts = 4 * s + k, slice(t * P, (t + 1) * P)
                        first, final = ks == 0, ks == KD - 1
                        nc.tensor.matmul(ps[:, t, :], h_hi[:, ks, ts], hi[:, k, :], start=first, stop=False)
                        nc.tensor.matmul(ps[:, t, :], h_lo[:, ks, ts], hi[:, k, :], start=False, stop=False)
                        ins = nc.tensor.matmul(ps[:, t, :], h_hi[:, ks, ts], lo[:, k, :], start=False,
                                               stop=final)
                ins.then_inc(chunk_done, 1)
            pair(0, MIXIN + 2, (4, 5), h_hi, h_lo)
            pe.wait_ge(v_gelu, NT)
            pair(1, MIXIN + 3, (0, 1), h_hi, h_lo)
            pair(0, MIXIN + 4, (2, 3), h_hi, h_lo)
            pe.wait_ge(xa_ready, KH)
            pair(1, MIXIN + 5, (4, 5), h_hi, h_lo)
            pe.wait_ge(mix_full, 16 * (3 + HEADS))
            for g in range(KH):
                pe.wait_ge(pooled_ready, g + 1)
                nc.tensor.matmul(ps[:, (6, 7, 0, 1)[g], :], wp[:, g, :], pooled[:, g, :], start=True,
                                 stop=True).then_inc(mixed, 1)
            pe.wait_ge(vn_ready, NT)
            pe.wait_ge(ws_ready, 2)
            for g in range(KH):
                pe.wait_ge(u_ready if g < 2 else y_ready, 2)
                for n in range(NT):
                    for i in range(2):
                        h = 2 * g + i
                        ins = nc.tensor.matmul(
                            ps[i * HC:(i + 1) * HC, (2, 3, 6, 7)[g], n * P:(n + 1) * P],
                            v_tok[:, n, h * HC:(h + 1) * HC], wsT[:, h, :], start=True, stop=True)
                ins.then_inc(spatial, 1)

            def y_block(k):
                pe.wait_ge(y_ready, k + 1)

            for q in range(KD // 2):
                if q == 0:
                    pe.wait_ge(y_ready, KH)
                elif q == 1:
                    pe.wait_ge(y32_ready, 2)
                else:
                    pe.wait_ge(x_new, KD + 2 * (q - 1))
                pair(q % 2, MIXOUT + q, (2 * (q % 2), 2 * (q % 2) + 1), y_hi, y_lo, y_block if q == 0 else None)
            sum_squares(2 * KD)

            up(UP2, 1, False)
            down(DOWN2, 1, 2 * KD, False, True)
            transpose_out(KD - 1)
            pe.wait_ge(sq_added, 3 * KD)
            pe.wait_ge(sq_ready, 3 * KD)
            for t in range(NT):
                ts = slice(t * P, (t + 1) * P)
                nc.tensor.matmul(ps[:, MOD, t:t + 1], work[:, 1, ts], ones[:, 0:1], start=True, stop=False)
                ins = nc.tensor.matmul(ps[:, MOD, t:t + 1], work[:, 0, ts], ones[:, 0:1], start=False, stop=True)
            ins.then_inc(sum_done, 1)


_INS = ["x", "c", "w_ada", "b_ada", "norm_ffn1_g", "ffn1_w_in", "ffn1_w_out", "norm_mix_g", "w_mix_in",
        "w_pool", "pool_scale", "gmlp_ln_g", "gmlp_ln_b", "w_spatial", "b_spatial", "w_mix_out",
        "norm_ffn2_g", "ffn2_w_in", "ffn2_w_out", "norm_final_g"]


def kernel(**inputs):
    import numpy as _np
    import concourse.bacc as _bacc
    from concourse import mybir as _mybir
    from concourse.bass_utils import run_bass_kernel_spmd as _run

    nc = _bacc.Bacc("TRN2", target_bir_lowering=False, num_devices=1)
    arrays, args = {}, []
    for name in _INS:
        a = _np.ascontiguousarray(inputs[name])
        arrays[f"in_{name}_dram"] = a
        args.append(nc.dram_tensor(f"in_{name}_dram", a.shape, _mybir.dt.from_np(a.dtype),
                                   kind="ExternalInput").ap())
    x = inputs["x"]
    args.append(nc.dram_tensor("out_dram", x.shape, _mybir.dt.from_np(_np.dtype(x.dtype)),
                               kind="ExternalOutput").ap())
    build_program(nc, *args)
    r = _run(nc, [arrays], core_ids=[0])
    return r.results[0]["out_dram"]
```

```python
from contextlib import ExitStack

import concourse.bass as bass
from concourse import mybir

P = 128
F32 = mybir.dt.float32
F32R = mybir.dt.float32r
ALU = mybir.AluOpType
ACT = mybir.ActivationFunctionType

EPS = 1e-6
HALF_STEP = 0.5
POOL_WINDOWS = (2, 4, 8, 16)
PAD = max(POOL_WINDOWS)


def build_program(nc, x, c, w_ada, b_ada, norm_ffn1_g, ffn1_w_in, ffn1_w_out, norm_mix_g, w_mix_in,
                  w_pool, pool_scale, gmlp_ln_g, gmlp_ln_b, w_spatial, b_spatial, w_mix_out,
                  norm_ffn2_g, ffn2_w_in, ffn2_w_out, norm_final_g, out):
    T, D = x.shape[1], x.shape[2]
    F = ffn1_w_out.shape[1]
    HEADS = w_spatial.shape[1]
    HC = D // 2 // HEADS
    KD, KF, KH = D // P, F // P, D // 2 // P
    NT = T // P
    NMOD = w_ada.shape[2] // P
    TILES = 2 * KD
    KC = KF // 2
    FULL, HALF = TILES * P, KC * P

    UP1 = 0
    DOWN1 = UP1 + KF
    MIXIN = DOWN1 + 2 * KD
    MIXOUT = MIXIN + 2 + KD // 2
    UP2 = MIXOUT + KD // 2
    DOWN2 = UP2 + KF
    END = DOWN2 + 2 * KD
    assert T == 512 and KF % 2 == 0 and D == 1024 and HEADS * HC == D // 2 and HC == 64

    FIRST = 2 * KD
    UNIT = 2 * P
    UNITS = (NMOD - FIRST) // 2
    assert KF < UNITS <= KF + KD and (UNITS - KF) % 2 == 0
    KA = KD // 2

    rows, at = {}, 0
    for name, n in (("b_ada", NMOD), ("g1", KD), ("gmix", KD), ("g2", KD), ("gfin", KD),
                    ("pool_scale", KH), ("c", KD)):
        rows[name] = at
        at += n
    NV = at

    ctx = ExitStack()
    with ctx:
        def sb(name, shape, dt=F32, scope=ctx):
            return scope.enter_context(nc.sbuf_tensor(name, shape, dt))

        def sem(name):
            return ctx.enter_context(nc.semaphore(name))

        xT = sb("xT", [P, KD, T])
        w_raw = sb("w_raw", [P, 2, FULL])
        w_hi = sb("w_hi", [P, 2, FULL], F32R)
        w_lo = sb("w_lo", [P, 2, FULL], F32R)
        ada_raw = sb("ada_raw", [P, 2, KA, UNIT])
        ada_acc = sb("ada_acc", [P, 2, UNIT])
        work = sb("work", [P, 3, T])
        ident = sb("ident", [P, P])
        ones = sb("ones", [P, P])
        vcol = sb("vcol", [P, NV])
        c_act = sb("c_act", [P, KD])
        mod = sb("mod", [P, NMOD])
        gs = sb("gs", [P, 3, KD])
        half_gate = sb("half_gate", [P, 2, KD])
        small = sb("small", [P, 64])

        with ExitStack() as over_h:
            vrow = sb("vrow", [P, P], F32, over_h)
        with ExitStack() as over_h:
            out_tok = sb("out_tok", [P, NT, D], F32, over_h)
        h_hi = sb("h_hi", [P, KD, T], F32R)
        h_lo = sb("h_lo", [P, KD, T], F32R)
        with ExitStack() as over_a:
            ada_first = sb("ada_first", [P, KD, FIRST * P], F32, over_a)
            acc_first = sb("acc_first", [P, FIRST * P], F32, over_a)
            x_tok = sb("x_tok", [P, NT, D], F32, over_a)
        with ExitStack() as over_a:
            y_hi = sb("y_hi", [P, KD, T], F32R, over_a)
            y_lo = sb("y_lo", [P, KD, T], F32R, over_a)
            v_tok = sb("v_tok", [P, NT, KH * P], F32, over_a)
            xa = sb("xa", [P, KH, PAD + T], F32, over_a)
            pooled = sb("pooled", [P, KH, T], F32, over_a)
            u_gelu = sb("u_gelu", [P, KH, T], F32, over_a)
            window = sb("window", [P, 2, PAD + T], F32, over_a)
            ln_g = sb("ln_g", [P, KH * P], F32, over_a)
            ln_b = sb("ln_b", [P, KH * P], F32, over_a)
            bias_t = sb("bias_t", [P, KH, P], F32, over_a)
            wp = sb("wp", [P, KH, P], F32, over_a)
            ws_raw = sb("ws_raw", [P, HEADS, P], F32, over_a)
            wsT = sb("wsT", [P, HEADS, P], F32, over_a)
        a_hi = sb("a_hi", [P, KF, T], F32R)
        a_lo = sb("a_lo", [P, KF, T], F32R)

        ps = ctx.enter_context(nc.psum_tensor("ps", [P, 8, T], F32))
        SUM, MOD = 6, 7

        mv = small[:, 0:2 * NT].rearrange("p (t s) -> p t s", s=2)
        rstd_in = small[:, 8:8 + NT]
        rstd = small[:, 12:12 + NT]
        minus_half = small[:, 16:16 + NT]
        inv_count = small[:, 20:20 + PAD]
        r_tok = small[:, 36:36 + NT]
        dummy = small[:, 40:41]
        eps_col = small[:, 41:42]
        stats = sb("stats", [P, NT, 6])

        raw_full = [sem("raw_full0"), sem("raw_full1")]
        hi_ready = sem("hi_ready")
        lo_ready = sem("lo_ready")
        chunk_done = sem("chunk_done")
        vec_full = sem("vec_full")
        x_full = sem("x_full")
        ws_full = sem("ws_full")
        first_full = [sem(f"first_full{k}") for k in range(KD)]
        ada_full = [sem("ada_full0"), sem("ada_full1")]
        mix_full = sem("mix_full")
        out_full = sem("out_full")
        consts = sem("consts")
        dve_const = sem("dve_const")
        ws_masked = sem("ws_masked")
        vec_T = sem("vec_T")
        vcol_ready = sem("vcol_ready")
        cact_ready = sem("cact_ready")
        first_step = sem("first_step")
        mod_done = sem("mod_done")
        mod_ready = sem("mod_ready")
        mod_link = sem("mod_link")
        x_T = sem("x_T")
        x_sq = sem("x_sq")
        ws_T = sem("ws_T")
        ws_ready = sem("ws_ready")
        sum_done = sem("sum_done")
        sq_summed = sem("sq_summed")
        root_ready = sem("root_ready")
        diag_ready = sem("diag_ready")
        r_spread = sem("r_spread")
        scaled = sem("scaled")
        h_hi_ready = sem("h_hi_ready")
        h_ready = sem("h_ready")
        silu_ready = sem("silu_ready")
        prod_ready = sem("prod_ready")
        a_hi_ready = sem("a_hi_ready")
        a_ready = sem("a_ready")
        ada_link = sem("ada_link")
        ada_summed = sem("ada_summed")
        x_new = sem("x_new")
        sq_ready = sem("sq_ready")
        sq_added = sem("sq_added")
        v_gelu = sem("v_gelu")
        ln_stat = sem("ln_stat")
        ln_eps = sem("ln_eps")
        ln_rstd = sem("ln_rstd")
        ln_link = sem("ln_link")
        vn_ready = sem("vn_ready")
        pads = sem("pads")
        xa_ready = sem("xa_ready")
        win_link = sem("win_link")
        win_ready = sem("win_ready")
        pooled_link = sem("pooled_link")
        pooled_ready = sem("pooled_ready")
        mixed = sem("mixed")
        y_hi_ready = sem("y_hi_ready")
        y_ready = sem("y_ready")
        u_ready = sem("u_ready")
        spatial = sem("spatial")
        gate_link = sem("gate_link")
        y32_ready = sem("y32_ready")
        yg_scaled = sem("yg_scaled")
        out_T = sem("out_T")
        out_copied = sem("out_copied")
        r_ready = sem("r_ready")
        y_out_dve = sem("y_out_dve")
        y_out_act = sem("y_out_act")

        def up_w(w):
            return w[0].rearrange("(k p) (s n) -> p k s n", p=P, s=2)

        def down_w(w):
            return w[0].rearrange("(s k p) n -> p s k n", p=P, s=2)

        def kpn(w):
            return w[0].rearrange("(k p) n -> p k n", p=P)

        w_ada_v = kpn(w_ada)

        def pair_view(ring, s):
            return ring[:, s].rearrange("p (s k n) -> p s k n", s=2, n=P)

        def half_view(ring, s):
            return ring[:, s, 0:HALF].rearrange("p (k n) -> p k n", n=P)

        def v_view(ring, s):
            return ring[:, s].rearrange("p (k n) -> p k n", n=KH * P)

        def mod_col(section, k):
            return mod[:, section * KD + k:section * KD + k + 1]

        def vec(name, k):
            return vcol[:, rows[name] + k:rows[name] + k + 1]

        block = ctx.enter_context(nc.Block())

        @block.sync
        def _(sp):
            def raw_free(chunk):
                if not (isinstance(chunk, int) and chunk < 2):
                    sp.wait_ge(lo_ready, chunk - 1)

            def load_pair(w, j, s, chunk):
                raw_free(chunk)
                for g in range(2):
                    sp.dma_start(pair_view(w_raw, s)[:, g], up_w(w)[:, :, g, bass.ds(j * P, P)])\
                      .then_inc(raw_full[s], 16)

            def load_two(w, col, s, chunk):
                raw_free(chunk)
                for g in range(2):
                    sp.dma_start(pair_view(w_raw, s)[:, g], kpn(w)[:, :, col + g * P:col + (g + 1) * P])\
                      .then_inc(raw_full[s], 16)

            def load_v(w, kq, s, chunk):
                raw_free(chunk)
                for g in range(2):
                    k0 = kq * 4 + 2 * g
                    sp.dma_start(v_view(w_raw, s)[:, 2 * g:2 * g + 2],
                                 kpn(w)[:, k0:k0 + 2, 2 * KH * P:3 * KH * P]).then_inc(raw_full[s], 16)

            def load_down(w, m, s, chunk):
                raw_free(chunk)
                for g, (k0, k1) in enumerate(((0, KC // 2), (KC // 2, KC))):
                    sp.dma_start(half_view(w_raw, s)[:, k0:k1], down_w(w)[:, s, k0:k1, bass.ds(m * P, P)])\
                      .then_inc(raw_full[s], 16)

            def load_ada(u):
                for s in range(2):
                    if not (isinstance(u, int) and u == 0):
                        sp.wait_ge(ada_link, u * KD - KA * (1 - s))
                    sp.dma_start(ada_raw[:, s], w_ada_v[:, s * KA:(s + 1) * KA,
                                                        bass.ds(u * UNIT + FIRST * P, UNIT)])\
                      .then_inc(ada_full[s], 16)

            def load_vec(name, v):
                n = v.shape[-1] // P
                sp.dma_start(vrow[rows[name]:rows[name] + n, :], v.rearrange("a (k p) -> (a k) p", p=P))\
                  .then_inc(vec_full, 16)

            def load_first(k):
                sp.dma_start(ada_first[:, k, :], w_ada_v[:, k, 0:FIRST * P]).then_inc(first_full[k], 16)

            load_vec("c", c)
            load_vec("b_ada", b_ada)
            load_first(0)
            for name, v in (("g1", norm_ffn1_g), ("gmix", norm_mix_g), ("g2", norm_ffn2_g),
                            ("gfin", norm_final_g.rearrange("(a d) -> a d", a=1)),
                            ("pool_scale", pool_scale)):
                load_vec(name, v)
            for t in range(NT):
                sp.dma_start(x_tok[:, t, :], x[0, t * P:(t + 1) * P, :]).then_inc(x_full, 16)
            for k in range(1, KD - 2):
                load_first(k)
            load_first(KD - 2)
            load_pair(ffn1_w_in, 0, 0, 0)
            load_first(KD - 1)
            load_pair(ffn1_w_in, 1, 1, 1)
            load_ada(0)

            for j in range(2):
                load_pair(ffn1_w_in, j + 2, j, UP1 + j + 2)
                load_ada(j + 1)
            with sp.Fori(1, KF // 2 - 1) as i:
                for s in range(2):
                    load_pair(ffn1_w_in, i * 2 + (s + 2), s, i * 2 + (s + 2 + UP1))
                    load_ada(i * 2 + (s + 1))
            load_ada(KF - 1)

            with sp.Fori(0, (UNITS - KF) // 2) as i:
                for q in range(2):
                    for s in range(2):
                        load_down(ffn1_w_out, i * 2 + q, s, i * 4 + 2 * q + s + DOWN1)
                    load_ada(i * 2 + q + KF)
            for m in range(UNITS - KF, KD):
                for s in range(2):
                    load_down(ffn1_w_out, m, s, DOWN1 + 2 * m + s)

            for s in range(2):
                load_v(w_mix_in, s, s, MIXIN + s)
            for q in range(2):
                load_two(w_mix_in, q * UNIT, q, MIXIN + 2 + q)
            sp.wait_ge(chunk_done, MIXIN)
            sp.dma_start(ws_raw[:], w_spatial[0].rearrange("h t s -> t h s")).then_inc(ws_full, 16)
            sp.dma_start(wp[:], w_pool[0].rearrange("g c d -> c g d")).then_inc(mix_full, 16)
            sp.dma_start(ln_g[:], gmlp_ln_g.to_broadcast([P, KH * P])).then_inc(mix_full, 16)
            sp.dma_start(ln_b[:], gmlp_ln_b.to_broadcast([P, KH * P])).then_inc(mix_full, 16)
            for h in range(HEADS):
                sp.dma_start(bias_t[(h % 2) * HC:(h % 2 + 1) * HC, h // 2, :],
                             b_spatial[0, h:h + 1, :].to_broadcast([HC, P])).then_inc(mix_full, 16)
            for q in range(2, 4):
                load_two(w_mix_in, q * UNIT, q % 2, MIXIN + 2 + q)
            for q in range(KD // 2):
                load_two(w_mix_out, q * UNIT, q % 2, MIXOUT + q)

            with sp.Fori(0, KF // 2) as i:
                for s in range(2):
                    load_pair(ffn2_w_in, i * 2 + s, s, i * 2 + s + UP2)
            with sp.Fori(0, KD) as m:
                for s in range(2):
                    load_down(ffn2_w_out, m, s, m * 2 + s + DOWN2)

            for t in (0, 1, 2, 3):
                if t == 1:
                    sp.wait_ge(y_out_act, 1)
                else:
                    sp.wait_ge(y_out_dve, max(t, 1))
                sp.dma_start(out[0, t * P:(t + 1) * P, :], out_tok[:, t, :]).then_inc(out_full, 16)
            sp.wait_ge(out_full, 16 * NT)

        @block.gpsimd
        def _(pool):
            nc.gpsimd.memset(ident[:], 0.0).then_inc(consts, 1)
            pool.wait_ge(consts, 1)
            nc.gpsimd.affine_select(out=ident[:], in_=ident[:], compare_op=ALU.not_equal, fill=1.0,
                                    base=0, pattern=[[-1, P]], channel_multiplier=1).then_inc(consts, 1)
            nc.gpsimd.memset(minus_half, -0.5).then_inc(consts, 1)

            pool.wait_ge(chunk_done, MIXIN)
            nc.gpsimd.memset(xa[:, :, 0:PAD], 0.0).then_inc(pads, 1)
            nc.gpsimd.memset(window[:, :, 0:PAD], 0.0).then_inc(pads, 1)
            pool.wait_ge(ws_full, 16)
            nc.gpsimd.affine_select(out=ws_raw[:], in_=ws_raw[:], compare_op=ALU.is_ge, fill=0.0,
                                    base=0, pattern=[[0, HEADS], [-1, P]], channel_multiplier=1)\
                .then_inc(ws_masked, 1)
            pool.wait_ge(ln_stat, NT)
            nc.gpsimd.tensor_scalar(rstd_in, mv[:, :, 1], EPS, 0.0, ALU.add, ALU.add).then_inc(ln_eps, 1)
            pool.wait_ge(ln_eps, 1)
            pool.wait_ge(consts, 3)
            nc.gpsimd.tensor_tensor(rstd, rstd_in, minus_half, ALU.pow).then_inc(ln_rstd, 1)
            link = 0
            for g, w in enumerate(POOL_WINDOWS):
                pool.wait_ge(xa_ready, g + 1)
                if g == 0:
                    pool.wait_ge(pads, 2)
                src, d, n = xa[:, g], 1, 0
                while d < w:
                    if g and n == 0:
                        pool.wait_ge(pooled_ready, g)
                    dst = window[:, n % 2]
                    ins = nc.gpsimd.tensor_tensor(dst[:, PAD:PAD + T], src[:, PAD:PAD + T],
                                                  src[:, PAD - d:PAD - d + T], ALU.add)
                    d *= 2
                    n += 1
                    src = dst
                    if d < w:
                        ins.then_inc(win_link, 1)
                        link += 1
                        pool.wait_ge(win_link, link)
                    else:
                        ins.then_inc(win_ready, 1)

        @block.scalar
        def _(act):
            def split_hi(s, n, chunk):
                number, half = (chunk, chunk // 2) if isinstance(chunk, int) else chunk
                act.wait_ge(raw_full[s], half * 32 + 32)
                if not (isinstance(number, int) and number < 2):
                    act.wait_ge(chunk_done, number - 1)
                nc.scalar.copy(w_hi[:, s, 0:n], w_raw[:, s, 0:n]).then_inc(hi_ready, 1)

            def h_his(count0, shift_section):
                for k in range(KD):
                    act.wait_ge(scaled, count0 + k + 1)
                    nc.scalar.activation(h_hi[:, k, :], work[:, k % 2, :], ACT.Identity,
                                         bias=mod_col(shift_section, k)).then_inc(h_hi_ready, 1)

            def root(n):
                act.wait_ge(sum_done, n)
                nc.scalar.activation(r_tok, ps[:, SUM if n < 4 else MOD, 0:NT], ACT.Sqrt, bias=eps_col,
                                     scale=1.0 / D).then_inc(root_ready, 1)

            act.wait_ge(dve_const, 2)
            act.wait_ge(vcol_ready, 1)
            nc.scalar.activation(c_act[:], vcol[:, rows["c"]:rows["c"] + KD], ACT.Silu).then_inc(cact_ready, 1)
            for k in range(KD):
                act.wait_ge(x_T, k + 1)
                nc.scalar.copy(xT[:, k, :], ps[:, k % 4, :])
                if k >= 2:
                    act.wait_ge(sq_summed, k - 1)
                nc.scalar.activation(work[:, k % 2, :], ps[:, k % 4, :], ACT.Square).then_inc(x_sq, 1)
            root(1)
            split_hi(0, FULL, 0)
            act.wait_ge(mod_ready, 1)
            h_his(0, 0)
            split_hi(1, FULL, 1)

            def up_step(j, jn, s, n_next, nxt):
                act.wait_ge(chunk_done, nxt[0] - 1)
                if not (isinstance(jn, int) and jn == 0):
                    act.wait_ge(prod_ready, jn)
                nc.scalar.activation(work[:, 0, :], ps[:, 2 * s, :], ACT.Silu).then_inc(silu_ready, 1)
                split_hi(s, n_next, nxt)
                act.wait_ge(prod_ready, jn + 1)
                nc.scalar.copy(a_hi[:, bass.ds(j, 1), :], work[:, 1:2, :]).then_inc(a_hi_ready, 1)

            def up(base, nth):
                for j in range(2):
                    up_step(j, j + nth * KF, j, FULL, (base + j + 2, base // 2 + 1))
                with act.Fori(1, KF // 2 - 1) as i:
                    for s in range(2):
                        up_step(i * 2 + s, i * 2 + (s + nth * KF), s, FULL,
                                (i * 2 + (s + base + 2), i + (base // 2 + 1)))
                for s in range(2):
                    j = KF - 2 + s
                    up_step(j, j + nth * KF, s, HALF, (base + j + 2, (base + j + 2) // 2))

            def square(m, x_count, added):
                act.wait_ge(x_new, x_count + 1)
                act.wait_ge(sq_added, added)
                src = xT[:, m, :] if isinstance(m, int) else xT[:, bass.ds(m, 1), :]
                dst = work[:, 0, :] if isinstance(m, int) else work[:, 0:1, :]
                nc.scalar.activation(dst, src, ACT.Square).then_inc(sq_ready, 1)

            def copy_out(m):
                act.wait_ge(out_T, m + 1)
                src = ps[:, SUM, :].rearrange("p (t f) -> p t f", t=NT)
                nc.scalar.copy(out_tok[:, :, bass.ds(m * P, P)], src).then_inc(out_copied, 1)

            def down(base, x_count, sq_count, last):
                nc.scalar.activation(dummy, ones[:, 0:1], ACT.Sqrt)
                with act.Fori(0, KD - 1) as m:
                    for s in range(2):
                        split_hi(s, HALF, (m * 2 + (base + s + 2), m + (base // 2 + 1)))
                    square(m, m + x_count, m + (sq_count + 1))
                    if last:
                        copy_out(m)
                if not last:
                    split_hi(0, FULL, base + 2 * KD)
                square(KD - 1, x_count + KD - 1, sq_count + KD)
                if last:
                    copy_out(KD - 1)

            up(UP1, 0)
            down(DOWN1, 0, 0, False)
            root(2)
            h_his(KD, 3)
            split_hi(1, FULL, MIXIN + 1)

            split_hi(0, FULL, MIXIN + 2)
            split_hi(1, FULL, MIXIN + 3)
            for t in range(NT):
                act.wait_ge(chunk_done, MIXIN + 2)
                nc.scalar.activation(v_tok[:, t, :], ps[:, t, :], ACT.Gelu_apprx_tanh).then_inc(v_gelu, 1)
            for q in range(2):
                act.wait_ge(ws_T, q + 1)
                nc.scalar.copy(wsT[:, 4 * q:4 * q + 4, :],
                               ps[:, 6 + q, :].rearrange("p (h t) -> p h t", h=4)).then_inc(ws_ready, 1)
            for q in range(2):
                act.wait_ge(chunk_done, MIXIN + 3 + q)
                for g in range(2):
                    nc.scalar.copy(xa[:, 2 * q + g, PAD:PAD + T], ps[:, (4, 5, 0, 1)[2 * q + g], :])\
                        .then_inc(xa_ready, 1)
                split_hi(q, FULL, MIXIN + 4 + q)
            for q in range(2):
                act.wait_ge(chunk_done, MIXIN + 5 + q)
                for g in range(2):
                    nc.scalar.activation(u_gelu[:, 2 * q + g, :], ps[:, (2, 3, 4, 5)[2 * q + g], :],
                                         ACT.Gelu_apprx_tanh).then_inc(u_ready, 1)
                if q == 0:
                    split_hi(0, FULL, MIXOUT)
            for g in range(KH):
                act.wait_ge(mixed, g + 1)
                nc.scalar.activation(y_hi[:, g, :], ps[:, (6, 7, 0, 1)[g], :], ACT.Identity,
                                     scale=vec("pool_scale", g)).then_inc(y_hi_ready, 1)
            split_hi(1, FULL, MIXOUT + 1)
            for g in range(KH):
                act.wait_ge(y32_ready, g + 1)
                nc.scalar.copy(y_hi[:, KH + g, :], pooled[:, g, :]).then_inc(y_hi_ready, 1)
            nc.scalar.activation(dummy, ones[:, 0:1], ACT.Sqrt)
            for q in range(KD // 2):
                if q < KD // 2 - 1:
                    split_hi(q % 2, FULL, MIXOUT + 2 + q)
                for g in range(2):
                    m = 2 * q + g
                    square(m, KD + m, KD + m + 1)
            root(3)
            h_his(2 * KD, 6)
            split_hi(1, FULL, UP2 + 1)

            up(UP2, 1)
            down(DOWN2, 2 * KD, 2 * KD, True)
            root(4)
            act.wait_ge(r_ready, 4)
            act.wait_ge(out_copied, KD)
            nc.scalar.activation(out_tok[:, 1, :], out_tok[:, 1, :], ACT.Copy,
                                 scale=r_tok[:, 1:2]).then_inc(y_out_act, 1)

        @block.vector
        def _(dve):
            def split_lo(s, n, number):
                dve.wait_ge(hi_ready, number + 1)
                nc.vector.tensor_tensor(w_lo[:, s, 0:n], w_raw[:, s, 0:n], w_hi[:, s, 0:n].bitcast(F32),
                                        ALU.subtract).then_inc(lo_ready, 1)

            def diagonal(n):
                dve.wait_ge(root_ready, n + 1)
                nc.vector.reciprocal(r_tok, r_tok).then_inc(r_ready, 1)
                dve.wait_ge(r_ready, n + 1)
                nc.vector.tensor_tensor(
                    work[:, 2, :].rearrange("p (t q) -> p t q", t=NT),
                    ident[:].rearrange("p (a q) -> p a q", a=1).to_broadcast([P, NT, P]),
                    r_tok.rearrange("p (t a) -> p t a", a=1).to_broadcast([P, NT, P]), ALU.mult)\
                    .then_inc(diag_ready, 1)

            def norm(n, count0, shift_section):
                dve.wait_ge(r_spread, n + 1)

                def lo(k):
                    dve.wait_ge(h_hi_ready, count0 + k + 1)
                    nc.vector.scalar_tensor_tensor(
                        h_lo[:, k, :], work[:, k % 2, :], mod_col(shift_section, k),
                        h_hi[:, k, :].bitcast(F32), ALU.add, ALU.subtract).then_inc(h_ready, 1)

                for k in range(KD):
                    if k >= 2:
                        dve.wait_ge(h_ready, count0 + k - 1)
                    nc.vector.scalar_tensor_tensor(work[:, k % 2, :], xT[:, k, :], gs[:, n, k:k + 1],
                                                   ps[:, SUM, :], ALU.mult, ALU.mult).then_inc(scaled, 1)
                    if k >= 1:
                        lo(k - 1)
                lo(KD - 1)

            def gains(n, name, scale_section):
                nc.vector.scalar_tensor_tensor(
                    gs[:, n, :], mod[:, scale_section * KD:(scale_section + 1) * KD], 1.0,
                    vcol[:, rows[name]:rows[name] + KD], ALU.add, ALU.mult).then_inc(mod_ready, 1)

            def take_mod(c0, c1, n):
                nc.vector.tensor_tensor(mod[:, c0:c1], ps[:, MOD, c0:c1],
                                        vcol[:, rows["b_ada"] + c0:rows["b_ada"] + c1], ALU.add)\
                    .then_inc(mod_link, 1)
                dve.wait_ge(mod_link, n)

            def ada_unit(u, s_acc):
                if not (isinstance(u, int) and u < 2):
                    dve.wait_ge(ada_summed, u - 1)
                for k in range(KD):
                    if k % KA == 0:
                        dve.wait_ge(ada_full[k // KA], u * 16 + 16)
                    w = ada_raw[:, k // KA, k % KA, :]
                    if k == 0:
                        ins = nc.vector.tensor_scalar(ada_acc[:, s_acc, :], w, c_act[:, 0:1], None, ALU.mult)
                    else:
                        dve.wait_ge(ada_link, u * KD + k)
                        ins = nc.vector.scalar_tensor_tensor(ada_acc[:, s_acc, :], w, c_act[:, k:k + 1],
                                                             ada_acc[:, s_acc, :], ALU.mult, ALU.add)
                    ins.then_inc(ada_link, 1)

            def up_step(j, jn, s, base, n_next, ada):
                if ada:
                    ada_unit(j, s)
                dve.wait_ge(silu_ready, jn + 1)
                if not (isinstance(jn, int) and jn == 0):
                    dve.wait_ge(a_ready, jn)
                nc.vector.tensor_tensor(work[:, 1, :], work[:, 0, :], ps[:, 2 * s + 1, :], ALU.mult)\
                    .then_inc(prod_ready, 1)
                split_lo(s, n_next, j + (base + 2))
                dve.wait_ge(a_hi_ready, jn + 1)
                if isinstance(j, int):
                    dst, prod, hi = a_lo[:, j, :], work[:, 1, :], a_hi[:, j, :]
                else:
                    dst, prod, hi = a_lo[:, bass.ds(j, 1), :], work[:, 1:2, :], a_hi[:, bass.ds(j, 1), :]
                nc.vector.tensor_tensor(dst, prod, hi.bitcast(F32), ALU.subtract).then_inc(a_ready, 1)

            def up(base, nth, ada):
                if ada:
                    for s in range(2):
                        up_step(s, s, s, base, FULL, ada)
                with dve.Fori(1 if ada else 0, KF // 2 - 1) as i:
                    for s in range(2):
                        up_step(i * 2 + s, i * 2 + (s + nth * KF), s, base, FULL, ada)
                for s in range(2):
                    j = KF - 2 + s
                    up_step(j, j + nth * KF, s, base, HALF, ada)

            def update(m, n_mm, bank, gate, x_dst):
                dve.wait_ge(chunk_done, n_mm)
                nc.vector.scalar_tensor_tensor(x_dst, ps[:, bank:bank + 1, :], gate, x_dst,
                                               ALU.mult, ALU.add).then_inc(x_new, 1)

            def add_squares(sq_n):
                dve.wait_ge(sq_ready, sq_n)
                nc.vector.tensor_tensor(work[:, 1, :], work[:, 1, :], work[:, 0, :], ALU.add)\
                    .then_inc(sq_added, 1)

            def final_gain(m, x_count):
                dve.wait_ge(x_new, x_count + 1)
                if not (isinstance(m, int) and m == 0):
                    dve.wait_ge(out_T, m)
                if isinstance(m, int):
                    src, g = xT[:, m, :], vec("gfin", m)
                else:
                    src, g = xT[:, bass.ds(m, 1), :], vcol[:, bass.ds(m + rows["gfin"], 1)]
                dst = work[:, 2, :] if isinstance(m, int) else work[:, 2:3, :]
                nc.vector.tensor_scalar(dst, src, g, None, ALU.mult).then_inc(yg_scaled, 1)

            def down(base, x_count, sq_count, gate_n, ada, last):
                dve.wait_ge(a_ready, (gate_n + 1) * KF)
                nc.vector.memset(work[:, 1, :], 0.0).then_inc(sq_added, 1)

                def block_of(m, bank, unit):
                    if unit is not None:
                        ada_unit(*unit)
                    if isinstance(m, int):
                        gate, x_dst = half_gate[:, gate_n, m:m + 1], xT[:, m:m + 1, :]
                    else:
                        gate, x_dst = half_gate[:, gate_n, bass.ds(m, 1)], xT[:, bass.ds(m, 1), :]
                    if not (isinstance(m, int) and m == KD - 1):
                        for s in range(2):
                            split_lo(s, HALF, m * 2 + (base + 2 + s))
                    elif not last:
                        split_lo(0, FULL, base + 2 * KD)
                    update(m, m * 2 + (base + 2), bank, gate, x_dst)
                    if last:
                        final_gain(m, m + x_count)
                    if not (isinstance(m, int) and m == KD - 1):
                        add_squares(m + (sq_count + 1))

                pairs = (UNITS - KF) // 2 if ada else KD // 2 - 1
                if last:
                    for q in range(2):
                        block_of(q, 4 + q, None)
                with dve.Fori(1 if last else 0, pairs) as i:
                    for q in range(2):
                        block_of(i * 2 + q, 4 + q, (i * 2 + (q + KF), q) if ada else None)
                for m in range(2 * pairs, KD):
                    block_of(m, 4 + m % 2, None)

            nc.vector.memset(ones[:], 1.0).then_inc(dve_const, 1)
            nc.vector.memset(eps_col, EPS).then_inc(dve_const, 1)
            for t in range(PAD):
                nc.vector.memset(inv_count[:, t:t + 1], 1.0 / (t + 1)).then_inc(dve_const, 1)
            dve.wait_ge(dve_const, 2 + PAD)
            dve.wait_ge(vec_T, 1)
            nc.vector.tensor_copy(vcol[:], ps[:, SUM, 0:NV]).then_inc(vcol_ready, 1)
            dve.wait_ge(cact_ready, 1)
            for k in range(KD - 1):
                if k == KD - 2:
                    dve.wait_ge(consts, 2)
                    diagonal(0)
                dve.wait_ge(first_full[k], 16)
                w = ada_first[:, k, :]
                if k == 0:
                    ins = nc.vector.tensor_scalar(acc_first[:], w, c_act[:, 0:1], None, ALU.mult)
                else:
                    dve.wait_ge(first_step, k)
                    ins = nc.vector.scalar_tensor_tensor(acc_first[:], w, c_act[:, k:k + 1], acc_first[:],
                                                         ALU.mult, ALU.add)
                ins.then_inc(first_step, 1)
            split_lo(0, FULL, 0)
            dve.wait_ge(mod_done, 1)
            take_mod(0, FIRST, 1)
            gains(0, "g1", 1)
            dve.wait_ge(mod_ready, 1)
            norm(0, 0, 0)
            split_lo(1, FULL, 1)

            up(UP1, 0, True)
            dve.wait_ge(ada_summed, KF - 1)
            take_mod(FIRST, FIRST + 2 * (KF - 1), 2)
            nc.vector.tensor_scalar(half_gate[:, 0, :], mod[:, 2 * KD:3 * KD], HALF_STEP, None, ALU.mult)\
                .then_inc(mod_ready, 1)
            dve.wait_ge(mod_ready, 2)
            down(DOWN1, 0, 0, 0, True, False)
            dve.wait_ge(ada_summed, UNITS)
            take_mod(FIRST + 2 * (KF - 1), NMOD, 3)
            gains(1, "gmix", 4)
            gains(2, "g2", 7)
            nc.vector.tensor_scalar(half_gate[:, 1, :], mod[:, 8 * KD:9 * KD], HALF_STEP, None, ALU.mult)\
                .then_inc(mod_ready, 1)
            dve.wait_ge(mod_ready, 5)
            diagonal(1)
            norm(1, KD, 3)
            split_lo(1, FULL, MIXIN + 1)

            for s in range(2):
                split_lo(s, FULL, MIXIN + 2 + s)
            for t in range(NT):
                dve.wait_ge(v_gelu, t + 1)
                nc.vector.bn_stats(stats[:, t, :], v_tok[:, t, :]).then_inc(ln_link, 1)
            for t in range(NT):
                dve.wait_ge(ln_link, t + 1)
                nc.vector.bn_aggr(mv[:, t, :], stats[:, t, :]).then_inc(ln_stat, 1)
            dve.wait_ge(ln_rstd, 1)
            for t in range(NT):
                nc.vector.tensor_scalar(v_tok[:, t, :], v_tok[:, t, :], mv[:, t, 0:1], rstd[:, t:t + 1],
                                        ALU.subtract, ALU.mult).then_inc(ln_link, 1)
            dve.wait_ge(mix_full, 16 * (3 + HEADS))
            for t in range(NT):
                dve.wait_ge(ln_link, NT + t + 1)
                nc.vector.tensor_tensor(v_tok[:, t, :], v_tok[:, t, :], ln_g[:], ALU.mult).then_inc(ln_link, 1)
            for t in range(NT):
                dve.wait_ge(ln_link, 2 * NT + t + 1)
                nc.vector.tensor_tensor(v_tok[:, t, :], v_tok[:, t, :], ln_b[:], ALU.add).then_inc(vn_ready, 1)
            split_lo(0, FULL, MIXIN + 4)
            for g, w in enumerate(POOL_WINDOWS):
                if g == 2:
                    split_lo(1, FULL, MIXIN + 5)
                dve.wait_ge(win_ready, g + 1)
                wsum = window[:, (w.bit_length() - 2) % 2]
                nc.vector.tensor_tensor(pooled[:, g, 0:w], wsum[:, PAD:PAD + w], inv_count[:, 0:w], ALU.mult)\
                    .then_inc(pooled_link, 1)
                nc.vector.scalar_tensor_tensor(pooled[:, g, w:T], wsum[:, PAD + w:PAD + T], 1.0 / w,
                                               xa[:, g, PAD + w:PAD + T], ALU.mult, ALU.subtract)\
                    .then_inc(pooled_link, 1)
                dve.wait_ge(pooled_link, 2 * g + 2)
                nc.vector.tensor_tensor(pooled[:, g, 0:w], pooled[:, g, 0:w], xa[:, g, PAD:PAD + w],
                                        ALU.subtract).then_inc(pooled_ready, 1)
            split_lo(0, FULL, MIXOUT)
            for g in range(KH):
                dve.wait_ge(y_hi_ready, g + 1)
                nc.vector.scalar_tensor_tensor(y_lo[:, g, :], ps[:, (6, 7, 0, 1)[g], :], vec("pool_scale", g),
                                               y_hi[:, g, :].bitcast(F32), ALU.mult, ALU.subtract)\
                    .then_inc(y_ready, 1)
            split_lo(1, FULL, MIXOUT + 1)
            for g in range(KH):
                dve.wait_ge(spatial, g + 1)
                dve.wait_ge(u_ready, g + 1)
                v3 = pooled[:, g, :].rearrange("p (n t) -> p n t", n=NT)
                sv3 = ps[:, (2, 3, 6, 7)[g], :].rearrange("p (n t) -> p n t", n=NT)
                b3 = bias_t[:, g:g + 1, :].to_broadcast([P, NT, P])
                nc.vector.tensor_tensor(v3, sv3, b3, ALU.add).then_inc(gate_link, 1)
                dve.wait_ge(gate_link, g + 1)
                nc.vector.tensor_tensor(pooled[:, g, :], pooled[:, g, :], u_gelu[:, g, :], ALU.mult)\
                    .then_inc(y32_ready, 1)
                if g:
                    dve.wait_ge(y_hi_ready, KH + g)
                    nc.vector.tensor_tensor(y_lo[:, KH + g - 1, :], pooled[:, g - 1, :],
                                            y_hi[:, KH + g - 1, :].bitcast(F32), ALU.subtract)\
                        .then_inc(y_ready, 1)
            dve.wait_ge(y_hi_ready, 2 * KH)
            nc.vector.tensor_tensor(y_lo[:, KD - 1, :], pooled[:, KH - 1, :],
                                    y_hi[:, KD - 1, :].bitcast(F32), ALU.subtract).then_inc(y_ready, 1)
            nc.vector.memset(work[:, 1, :], 0.0).then_inc(sq_added, 1)
            for q in range(KD // 2):
                if q < KD // 2 - 1:
                    split_lo(q % 2, FULL, MIXOUT + 2 + q)
                for g in range(2):
                    m = 2 * q + g
                    update(m, MIXOUT + q + 1, 2 * (q % 2) + g, mod_col(5, m), xT[:, m:m + 1, :])
                    if m < KD - 1:
                        add_squares(KD + m + 1)
            diagonal(2)
            norm(2, 2 * KD, 6)
            split_lo(1, FULL, UP2 + 1)

            up(UP2, 1, False)
            down(DOWN2, 2 * KD, 2 * KD, 1, False, True)
            dve.wait_ge(root_ready, 4)
            nc.vector.reciprocal(r_tok, r_tok).then_inc(r_ready, 1)
            dve.wait_ge(r_ready, 4)
            dve.wait_ge(out_copied, KD)
            for t in (0, 2, 3):
                nc.vector.tensor_scalar(out_tok[:, t, :], out_tok[:, t, :], r_tok[:, t:t + 1], None, ALU.mult)\
                    .then_inc(y_out_dve, 1)

        @block.tensor
        def _(pe):
            def product(dst, w_h, w_l, a_h, a_l, start, stop):
                nc.tensor.matmul(dst, w_h, a_h, start=start, stop=False)
                nc.tensor.matmul(dst, w_l, a_h, start=False, stop=False)
                return nc.tensor.matmul(dst, w_h, a_l, start=False, stop=stop)

            def pair(s, number, banks, src_hi, src_lo, wait_k=None):
                pe.wait_ge(lo_ready, number + 1)
                hi, lo = pair_view(w_hi, s), pair_view(w_lo, s)
                for k in range(KD):
                    if wait_k:
                        wait_k(k)
                    for g in range(2):
                        ins = product(ps[:, banks[g], :], hi[:, g, k, :], lo[:, g, k, :],
                                      src_hi[:, k, :], src_lo[:, k, :], k == 0, k == KD - 1)
                ins.then_inc(chunk_done, 1)

            def sum_unit(u, s):
                pe.wait_ge(ada_link, u * KD + KD)
                for t in range(2):
                    if isinstance(u, int):
                        col = FIRST + 2 * u + t
                        dst = ps[:, MOD, col:col + 1]
                    else:
                        dst = ps[:, MOD, bass.ds(u * 2 + (FIRST + t), 1)]
                    ins = nc.tensor.matmul(dst, ada_acc[:, s, t * P:(t + 1) * P], ones[:, 0:1],
                                           start=True, stop=True)
                ins.then_inc(ada_summed, 1)

            def up(base, nth, ada):
                def h_block(k):
                    pe.wait_ge(h_ready, (2 * nth) * KD + k + 1)

                def step(j, s, wait_k=None):
                    if not (isinstance(j, int) and j < 2):
                        pe.wait_ge(prod_ready, j + (nth * KF - 1))
                    pair(s, j + base, (2 * s, 2 * s + 1), h_hi, h_lo, wait_k)
                    if ada and not (isinstance(j, int) and j == 0):
                        sum_unit(j - 1, 1 - s)

                step(0, 0, h_block)
                step(1, 1)
                with pe.Fori(1, KF // 2) as i:
                    for s in range(2):
                        step(i * 2 + s, s)

            def down(base, gate_n, x_count, ada, last):
                def block_of(m, bank):
                    if not (isinstance(m, int) and m < 2):
                        pe.wait_ge(x_new, m + (x_count - 1))
                    for s in range(2):
                        pe.wait_ge(lo_ready, m * 2 + (base + s + 1))
                        pe.wait_ge(a_ready, gate_n * KF + (KC if s == 0 else KF))
                        hi, lo = half_view(w_hi, s), half_view(w_lo, s)
                        for k in range(KC):
                            ins = product(ps[:, bank, :], hi[:, k, :], lo[:, k, :],
                                          a_hi[:, s * KC + k, :], a_lo[:, s * KC + k, :],
                                          s == 0 and k == 0, s == 1 and k == KC - 1)
                        ins.then_inc(chunk_done, 1)
                        if last and s == 0 and not (isinstance(m, int) and m == 0):
                            transpose_out(m - 1)
                    if ada and isinstance(m, int) and m == 0:
                        pe.wait_ge(mod_ready, 2)
                    if ada and not (isinstance(m, int) and KF + m > UNITS):
                        sum_unit(m + (KF - 1), 1 - bank % 2)

                for m in range(2):
                    block_of(m, 4 + m)
                with pe.Fori(1, KD // 2 - 1) as i:
                    for q in range(2):
                        block_of(i * 2 + q, 4 + q)
                for m in range(KD - 2, KD):
                    block_of(m, 4 + m % 2)

            def transpose_out(m):
                pe.wait_ge(yg_scaled, m + 1)
                if not (isinstance(m, int) and m == 0):
                    pe.wait_ge(out_copied, m)
                for t in range(NT):
                    ins = nc.tensor.transpose(ps[:, SUM, t * P:(t + 1) * P], work[:, 2, t * P:(t + 1) * P],
                                              ident[:])
                ins.then_inc(out_T, 1)

            def sum_columns(bank, src, start, stop):
                for t in range(NT):
                    ins = nc.tensor.matmul(ps[:, bank, t:t + 1], work[:, src, t * P:(t + 1) * P],
                                           ones[:, 0:1], start=start and t == 0, stop=stop and t == NT - 1,
                                           skip_group_check=True)
                return ins

            def sum_squares(sq_n, bank):
                pe.wait_ge(sq_added, sq_n)
                sum_columns(bank, 1, True, False)
                pe.wait_ge(sq_ready, sq_n)
                sum_columns(bank, 0, False, True).then_inc(sum_done, 1)

            def spread(n):
                pe.wait_ge(diag_ready, n + 1)
                nc.tensor.matmul(ps[:, SUM, :], ones[:], work[:, 2, :], start=True, stop=True)\
                    .then_inc(r_spread, 1)

            pe.wait_ge(consts, 2)
            pe.wait_ge(vec_full, 16 * len(rows))
            nc.tensor.transpose(ps[:, SUM, 0:NV], vrow[0:NV, :], ident[0:NV, 0:NV]).then_inc(vec_T, 1)
            pe.wait_ge(x_full, 16 * NT)
            pe.wait_ge(dve_const, 1)
            pe.wait_ge(vcol_ready, 1)

            def sum_x(k):
                pe.wait_ge(x_sq, k + 1)
                sum_columns(SUM, k % 2, k == 0, k == KD - 1).then_inc(sq_summed if k < KD - 1 else sum_done, 1)

            for k in range(KD):
                if k >= 4:
                    pe.wait_ge(x_sq, k - 3)
                for t in range(NT):
                    ins = nc.tensor.transpose(ps[:, k % 4, t * P:(t + 1) * P],
                                              x_tok[:, t, k * P:(k + 1) * P], ident[:])
                ins.then_inc(x_T, 1)
                if k >= 1:
                    sum_x(k - 1)
            sum_x(KD - 1)
            spread(0)
            pe.wait_ge(first_step, KD - 1)
            for col in range(FIRST):
                nc.tensor.matmul(ps[:, MOD, col:col + 1], acc_first[:, col * P:(col + 1) * P],
                                 ones[:, 0:1], start=col == 0, stop=False, skip_group_check=True)
            pe.wait_ge(first_full[KD - 1], 16)
            for col in range(FIRST):
                ins = nc.tensor.matmul(ps[:, MOD, col:col + 1], ada_first[:, KD - 1, col * P:(col + 1) * P],
                                       c_act[:, KD - 1:KD], start=False, stop=col == FIRST - 1,
                                       skip_group_check=True)
            ins.then_inc(mod_done, 1)
            pe.wait_ge(mod_ready, 1)

            up(UP1, 0, True)
            down(DOWN1, 0, 0, True, False)
            sum_squares(KD, SUM)
            spread(1)

            for s in range(2):
                pe.wait_ge(lo_ready, MIXIN + s + 1)
                hi, lo = v_view(w_hi, s), v_view(w_lo, s)
                for k in range(4):
                    pe.wait_ge(h_ready, KD + 4 * s + k + 1)
                    for t in range(NT):
                        ks, ts = 4 * s + k, slice(t * P, (t + 1) * P)
                        first, final = ks == 0, ks == KD - 1
                        nc.tensor.matmul(ps[:, t, :], h_hi[:, ks, ts], hi[:, k, :], start=first, stop=False)
                        nc.tensor.matmul(ps[:, t, :], h_lo[:, ks, ts], hi[:, k, :], start=False, stop=False)
                        ins = nc.tensor.matmul(ps[:, t, :], h_hi[:, ks, ts], lo[:, k, :], start=False,
                                               stop=final)
                ins.then_inc(chunk_done, 1)
            pe.wait_ge(ws_masked, 1)
            for q in range(2):
                for h in range(4):
                    ins = nc.tensor.transpose(ps[:, 6 + q, h * P:(h + 1) * P], ws_raw[:, 4 * q + h, :], ident[:])
                ins.then_inc(ws_T, 1)
            pair(0, MIXIN + 2, (4, 5), h_hi, h_lo)
            pe.wait_ge(v_gelu, NT)
            pair(1, MIXIN + 3, (0, 1), h_hi, h_lo)
            pair(0, MIXIN + 4, (2, 3), h_hi, h_lo)
            pe.wait_ge(xa_ready, KH)
            pair(1, MIXIN + 5, (4, 5), h_hi, h_lo)
            pe.wait_ge(mix_full, 16 * (3 + HEADS))
            pe.wait_ge(ws_ready, 2)
            for g in range(KH):
                pe.wait_ge(pooled_ready, g + 1)
                nc.tensor.matmul(ps[:, (6, 7, 0, 1)[g], :], wp[:, g, :], pooled[:, g, :], start=True,
                                 stop=True).then_inc(mixed, 1)
            pe.wait_ge(vn_ready, NT)
            for g in range(KH):
                pe.wait_ge(u_ready if g < 2 else y_ready, 2)
                for n in range(NT):
                    for i in range(2):
                        h = 2 * g + i
                        ins = nc.tensor.matmul(
                            ps[i * HC:(i + 1) * HC, (2, 3, 6, 7)[g], n * P:(n + 1) * P],
                            v_tok[:, n, h * HC:(h + 1) * HC], wsT[:, h, :], start=True, stop=True)
                ins.then_inc(spatial, 1)

            def y_block(k):
                pe.wait_ge(y_ready, k + 1)

            for q in range(KD // 2):
                if q == 0:
                    pe.wait_ge(y_ready, KH)
                elif q == 1:
                    pe.wait_ge(y32_ready, 2)
                else:
                    pe.wait_ge(x_new, KD + 2 * (q - 1))
                pair(q % 2, MIXOUT + q, (2 * (q % 2), 2 * (q % 2) + 1), y_hi, y_lo, y_block if q == 0 else None)
            sum_squares(2 * KD, SUM)
            spread(2)

            up(UP2, 1, False)
            down(DOWN2, 1, 2 * KD, False, True)
            transpose_out(KD - 1)
            sum_squares(3 * KD, MOD)


_INS = ["x", "c", "w_ada", "b_ada", "norm_ffn1_g", "ffn1_w_in", "ffn1_w_out", "norm_mix_g", "w_mix_in",
        "w_pool", "pool_scale", "gmlp_ln_g", "gmlp_ln_b", "w_spatial", "b_spatial", "w_mix_out",
        "norm_ffn2_g", "ffn2_w_in", "ffn2_w_out", "norm_final_g"]


def kernel(**inputs):
    import numpy as _np
    import concourse.bacc as _bacc
    from concourse import mybir as _mybir
    from concourse.bass_utils import run_bass_kernel_spmd as _run

    nc = _bacc.Bacc("TRN2", target_bir_lowering=False, num_devices=1)
    arrays, args = {}, []
    for name in _INS:
        a = _np.ascontiguousarray(inputs[name])
        arrays[f"in_{name}_dram"] = a
        args.append(nc.dram_tensor(f"in_{name}_dram", a.shape, _mybir.dt.from_np(a.dtype),
                                   kind="ExternalInput").ap())
    x = inputs["x"]
    args.append(nc.dram_tensor("out_dram", x.shape, _mybir.dt.from_np(_np.dtype(x.dtype)),
                               kind="ExternalOutput").ap())
    build_program(nc, *args)
    r = _run(nc, [arrays], core_ids=[0])
    return r.results[0]["out_dram"]
```

```python
from contextlib import ExitStack

import concourse.bass as bass
from concourse import mybir

P = 128
F32 = mybir.dt.float32
F32R = mybir.dt.float32r
ALU = mybir.AluOpType
ACT = mybir.ActivationFunctionType

EPS = 1e-6
HALF_STEP = 0.5
POOL_WINDOWS = (2, 4, 8, 16)
PAD = max(POOL_WINDOWS)


def build_program(nc, x, c, w_ada, b_ada, norm_ffn1_g, ffn1_w_in, ffn1_w_out, norm_mix_g, w_mix_in,
                  w_pool, pool_scale, gmlp_ln_g, gmlp_ln_b, w_spatial, b_spatial, w_mix_out,
                  norm_ffn2_g, ffn2_w_in, ffn2_w_out, norm_final_g, out):
    T, D = x.shape[1], x.shape[2]
    F = ffn1_w_out.shape[1]
    HEADS = w_spatial.shape[1]
    HC = D // 2 // HEADS
    KD, KF, KH = D // P, F // P, D // 2 // P
    NT = T // P
    NMOD = w_ada.shape[2] // P
    TILES = 2 * KD
    KC = KF // 2
    FULL, HALF = TILES * P, KC * P

    UP1 = 0
    DOWN1 = UP1 + KF
    MIXIN = DOWN1 + 2 * KD
    MIXOUT = MIXIN + 2 + KD // 2
    UP2 = MIXOUT + KD // 2
    DOWN2 = UP2 + KF
    END = DOWN2 + 2 * KD
    assert T == 512 and KF % 2 == 0 and D == 1024 and HEADS * HC == D // 2 and HC == 64

    FIRST = 2 * KD
    UNIT = 2 * P
    UNITS = (NMOD - FIRST) // 2
    assert KF < UNITS <= KF + KD and (UNITS - KF) % 2 == 0
    Q = 32
    LINKS = KD + 2
    KA = KD // 2
    LAG = 2
    POOL_K, DVE_K = 3, 4

    TH = T // 2
    HALVES = (slice(0, TH), slice(TH, T))
    LAST_BANK = (5, 3)
    MIX_LAST = ((2, 3), (5, 6))
    SPREAD = {1: (4, 6), 2: (4, 2)}

    def steps_of(ks, half):
        return [(k, slice(0, T) if half is None else HALVES[half], half) for k in ks]

    STEPS = {0: steps_of(range(KD), None),
             1: steps_of(range(KD // 2), 0) + steps_of(range(KD // 2), 1) + steps_of(range(KD // 2, KD), None),
             2: steps_of(range(KD), 0) + steps_of(range(KD), 1)}
    SCALED = (0, 1, 3, 4)
    LONG_LAG = {1: KD * KD, 2: KD + 2}
    H_AT = {0: 0, 1: KD, 2: KD + len(STEPS[1])}
    X_AT = {0: 0, 1: KD - 1, 2: 2 * KD - 3}
    SQ_AT = {0: 0, 1: KD, 2: 2 * KD - 1}
    LAST_AT = {0: 0, 1: 2, 2: 6}
    LAST_SQ = {1: (1, 2), 2: (4, 6), 3: (7, 8)}

    rows, at = {}, 0
    for name, n in (("b_ada", NMOD), ("g1", KD), ("gmix", KD), ("g2", KD), ("gfin", KD),
                    ("pool_scale", KH), ("c", KD)):
        rows[name] = at
        at += n
    NV = at

    ctx = ExitStack()
    with ctx:
        def sb(name, shape, dt=F32, scope=ctx):
            return scope.enter_context(nc.sbuf_tensor(name, shape, dt))

        def sem(name):
            return ctx.enter_context(nc.semaphore(name))

        xT = sb("xT", [P, KD, T])
        w_raw = sb("w_raw", [P, 2, FULL])
        w_hi = sb("w_hi", [P, 2, FULL], F32R)
        w_lo = sb("w_lo", [P, 2, FULL], F32R)
        ada_raw = sb("ada_raw", [P, 2, KA, UNIT])
        ada_acc = sb("ada_acc", [P, UNIT])
        ada_T = sb("ada_T", [P, UNIT])
        ada_part = sb("ada_part", [P, UNITS, UNIT // Q])
        fold = sb("fold", [P, P])
        work = sb("work", [P, 5, T])
        ident = sb("ident", [P, P])
        ones = sb("ones", [P, P])
        vcol = sb("vcol", [P, NV])
        c_act = sb("c_act", [P, KD])
        mod = sb("mod", [P, NMOD])
        gs = sb("gs", [P, 3, KD])
        half_gate = sb("half_gate", [P, 2, KD])
        small = sb("small", [P, 64])

        with ExitStack() as over_h:
            vrow = sb("vrow", [P, P], F32, over_h)
        with ExitStack() as over_h:
            out_tok = sb("out_tok", [P, NT, D], F32, over_h)
        h_hi = sb("h_hi", [P, KD, T], F32R)
        h_lo = sb("h_lo", [P, KD, T], F32R)
        with ExitStack() as over_a:
            ada_first = sb("ada_first", [P, KD, 2, KD, P], F32, over_a)
            acc_first = sb("acc_first", [P, KD, 2, P], F32, over_a)
            x_tok = sb("x_tok", [P, NT, D], F32, over_a)
        with ExitStack() as over_a:
            y_hi = sb("y_hi", [P, KD, T], F32R, over_a)
            y_lo = sb("y_lo", [P, KD, T], F32R, over_a)
            v_tok = sb("v_tok", [P, NT, KH * P], F32, over_a)
            xa = sb("xa", [P, KH, PAD + T], F32, over_a)
            pooled = sb("pooled", [P, KH, T], F32, over_a)
            u_gelu = sb("u_gelu", [P, KH, T], F32, over_a)
            window = sb("window", [P, 2, PAD + T], F32, over_a)
            ln_g = sb("ln_g", [P, KH * P], F32, over_a)
            ln_b = sb("ln_b", [P, KH * P], F32, over_a)
            bias_t = sb("bias_t", [P, KH, P], F32, over_a)
            wp = sb("wp", [P, KH, P], F32, over_a)
            ws_raw = sb("ws_raw", [P, HEADS, P], F32, over_a)
            wsT = sb("wsT", [P, HEADS, P], F32, over_a)
        a_hi = sb("a_hi", [P, KF, T], F32R)
        a_lo = sb("a_lo", [P, KF, T], F32R)

        ps = ctx.enter_context(nc.psum_tensor("ps", [P, 8, T], F32))
        SUM, MOD = 6, 7
        MOD_ODD = 5

        mv = small[:, 0:2 * NT].rearrange("p (t s) -> p t s", s=2)
        rstd_in = small[:, 8:8 + NT]
        rstd = small[:, 12:12 + NT]
        minus_half = small[:, 16:16 + NT]
        inv_count = small[:, 20:20 + PAD]
        r_tok = small[:, 36:36 + NT]
        dummy = small[:, 40:41]
        eps_col = small[:, 41:42]
        sum_tok = small[:, 42:42 + NT]
        stats = sb("stats", [P, NT, 6])

        raw_full = [sem("raw_full0"), sem("raw_full1")]
        hi_half = sem("hi_half")
        hi_ready = sem("hi_ready")
        lo_ready = sem("lo_ready")
        chunk_done = sem("chunk_done")
        vec_full = sem("vec_full")
        x_full = [sem(f"x_full{t}") for t in range(NT)]
        ws_full = sem("ws_full")
        first_full = [sem(f"first_full{k}") for k in range(KD)]
        ada_full = [sem("ada_full0"), sem("ada_full1")]
        mix_full = sem("mix_full")
        out_full = sem("out_full")
        consts = sem("consts")
        dve_const = sem("dve_const")
        ws_masked = sem("ws_masked")
        vec_T = sem("vec_T")
        vcol_ready = sem("vcol_ready")
        cact_ready = sem("cact_ready")
        first_step = sem("first_step")
        pool_step = sem("pool_step")
        lo_half = sem("lo_half")
        first_summed = sem("first_summed")
        first_taken = sem("first_taken")
        first_gain = sem("first_gain")
        mod_ready = sem("mod_ready")
        mod_link = sem("mod_link")
        x_T = sem("x_T")
        x_sq = sem("x_sq")
        x_even = sem("x_even")
        x_odd = sem("x_odd")
        ws_T = sem("ws_T")
        ws_ready = sem("ws_ready")
        sum_done = sem("sum_done")
        root_ready = sem("root_ready")
        diag_ready = sem("diag_ready")
        r_spread = sem("r_spread")
        scaled = sem("scaled")
        h_hi_ready = sem("h_hi_ready")
        h_ready = sem("h_ready")
        silu_ready = sem("silu_ready")
        prod_ready = sem("prod_ready")
        a_hi_ready = sem("a_hi_ready")
        a_ready = sem("a_ready")
        ada_link = sem("ada_link")
        ada_summed = sem("ada_summed")
        x_new = sem("x_new")
        sq_ready = sem("sq_ready")
        sq_added = sem("sq_added")
        v_gelu = sem("v_gelu")
        ln_stat = sem("ln_stat")
        ln_eps = sem("ln_eps")
        ln_rstd = sem("ln_rstd")
        ln_link = sem("ln_link")
        vn_ready = sem("vn_ready")
        pads = sem("pads")
        xa_ready = sem("xa_ready")
        win_link = sem("win_link")
        win_ready = sem("win_ready")
        pooled_link = sem("pooled_link")
        pooled_ready = sem("pooled_ready")
        mixed = sem("mixed")
        y_hi_ready = sem("y_hi_ready")
        y_ready = sem("y_ready")
        u_ready = sem("u_ready")
        spatial = sem("spatial")
        gate_link = sem("gate_link")
        y32_ready = sem("y32_ready")
        yg_scaled = sem("yg_scaled")
        last_done = sem("last_done")
        last_new = sem("last_new")
        last_sq = sem("last_sq")
        out_T = sem("out_T")
        out_copied = sem("out_copied")
        r_ready = sem("r_ready")
        y_out_dve = sem("y_out_dve")
        y_out_act = sem("y_out_act")

        def up_w(w):
            return w[0].rearrange("(k p) (s n) -> p k s n", p=P, s=2)

        def down_w(w):
            return w[0].rearrange("(s k p) n -> p s k n", p=P, s=2)

        def kpn(w):
            return w[0].rearrange("(k p) n -> p k n", p=P)

        w_ada_v = kpn(w_ada)

        def pair_view(ring, s):
            return ring[:, s].rearrange("p (s k n) -> p s k n", s=2, n=P)

        def half_view(ring, s):
            return ring[:, s, 0:HALF].rearrange("p (k n) -> p k n", n=P)

        def v_view(ring, s):
            return ring[:, s].rearrange("p (k n) -> p k n", n=KH * P)

        def mod_col(section, k):
            return mod[:, section * KD + k:section * KD + k + 1]

        def vec(name, k):
            return vcol[:, rows[name] + k:rows[name] + k + 1]

        block = ctx.enter_context(nc.Block())

        @block.sync
        def _(sp):
            def raw_free(chunk):
                if not (isinstance(chunk, int) and chunk < 2):
                    sp.wait_ge(lo_ready, chunk - 1)

            def load_pair(w, j, s, chunk):
                raw_free(chunk)
                for g in range(2):
                    sp.dma_start(pair_view(w_raw, s)[:, g], up_w(w)[:, :, g, bass.ds(j * P, P)])\
                      .then_inc(raw_full[s], 16)

            def load_two(w, col, s, chunk):
                raw_free(chunk)
                for g in range(2):
                    sp.dma_start(pair_view(w_raw, s)[:, g], kpn(w)[:, :, col + g * P:col + (g + 1) * P])\
                      .then_inc(raw_full[s], 16)

            def load_v(w, kq, s, chunk):
                raw_free(chunk)
                for g in range(2):
                    k0 = kq * 4 + 2 * g
                    sp.dma_start(v_view(w_raw, s)[:, 2 * g:2 * g + 2],
                                 kpn(w)[:, k0:k0 + 2, 2 * KH * P:3 * KH * P]).then_inc(raw_full[s], 16)

            def load_down(w, m, s, chunk):
                raw_free(chunk)
                for g, (k0, k1) in enumerate(((0, KC // 2), (KC // 2, KC))):
                    sp.dma_start(half_view(w_raw, s)[:, k0:k1], down_w(w)[:, s, k0:k1, bass.ds(m * P, P)])\
                      .then_inc(raw_full[s], 16)

            def load_ada(u):
                for s in range(2):
                    if not (isinstance(u, int) and u == 0):
                        sp.wait_ge(ada_link, u * LINKS - (LINKS - KA * (s + 1)))
                    sp.dma_start(ada_raw[:, s], w_ada_v[:, s * KA:(s + 1) * KA,
                                                        bass.ds(u * UNIT + FIRST * P, UNIT)])\
                      .then_inc(ada_full[s], 16)

            def load_vec(name, v):
                n = v.shape[-1] // P
                sp.dma_start(vrow[rows[name]:rows[name] + n, :], v.rearrange("a (k p) -> (a k) p", p=P))\
                  .then_inc(vec_full, 16)

            def load_first(k):
                for sec in range(2):
                    col = (sec * KD + k) * P
                    sp.dma_start(ada_first[:, k, sec], w_ada_v[:, :, col:col + P]).then_inc(first_full[k], 16)

            def load_x(t):
                sp.dma_start(x_tok[:, t, :], x[0, t * P:(t + 1) * P, :]).then_inc(x_full[t], 16)

            load_x(0)
            load_vec("c", c)
            load_vec("b_ada", b_ada)
            load_x(1)
            load_vec("g1", norm_ffn1_g)
            load_vec("gmix", norm_mix_g)
            load_x(2)
            load_vec("g2", norm_ffn2_g)
            load_vec("gfin", norm_final_g.rearrange("(a d) -> a d", a=1))
            load_x(3)
            load_vec("pool_scale", pool_scale)
            load_first(0)
            load_pair(ffn1_w_in, 0, 0, 0)
            load_first(1)
            load_pair(ffn1_w_in, 1, 1, 1)
            for k in range(2, KD):
                load_first(k)
            load_ada(0)

            for j in range(2):
                load_pair(ffn1_w_in, j + 2, j, UP1 + j + 2)
                load_ada(j + 1)
            with sp.Fori(1, KF // 2 - 1) as i:
                for s in range(2):
                    load_pair(ffn1_w_in, i * 2 + (s + 2), s, i * 2 + (s + 2 + UP1))
                    load_ada(i * 2 + (s + 1))
            load_ada(KF - 1)

            with sp.Fori(0, (UNITS - KF) // 2) as i:
                for q in range(2):
                    for s in range(2):
                        load_down(ffn1_w_out, i * 2 + q, s, i * 4 + 2 * q + s + DOWN1)
                    load_ada(i * 2 + q + KF)
            for m in range(UNITS - KF, KD):
                for s in range(2):
                    load_down(ffn1_w_out, m, s, DOWN1 + 2 * m + s)

            for s in range(2):
                load_v(w_mix_in, s, s, MIXIN + s)
            for q in range(2):
                load_two(w_mix_in, q * UNIT, q, MIXIN + 2 + q)
            sp.wait_ge(chunk_done, MIXIN)
            sp.dma_start(ws_raw[:], w_spatial[0].rearrange("h t s -> t h s")).then_inc(ws_full, 16)
            sp.dma_start(wp[:], w_pool[0].rearrange("g c d -> c g d")).then_inc(mix_full, 16)
            sp.dma_start(ln_g[:], gmlp_ln_g.to_broadcast([P, KH * P])).then_inc(mix_full, 16)
            sp.dma_start(ln_b[:], gmlp_ln_b.to_broadcast([P, KH * P])).then_inc(mix_full, 16)
            for h in range(HEADS):
                sp.dma_start(bias_t[(h % 2) * HC:(h % 2 + 1) * HC, h // 2, :],
                             b_spatial[0, h:h + 1, :].to_broadcast([HC, P])).then_inc(mix_full, 16)
            for q in range(2, 4):
                load_two(w_mix_in, q * UNIT, q % 2, MIXIN + 2 + q)
            for q in range(KD // 2):
                load_two(w_mix_out, q * UNIT, q % 2, MIXOUT + q)

            with sp.Fori(0, KF // 2) as i:
                for s in range(2):
                    load_pair(ffn2_w_in, i * 2 + s, s, i * 2 + s + UP2)
            with sp.Fori(0, KD) as m:
                for s in range(2):
                    load_down(ffn2_w_out, m, s, m * 2 + s + DOWN2)

            for t in range(NT):
                sp.wait_ge(y_out_act if t % 2 else y_out_dve, t // 2 + 1)
                sp.dma_start(out[0, t * P:(t + 1) * P, :], out_tok[:, t, :]).then_inc(out_full, 16)
            sp.wait_ge(out_full, 16 * NT)

        @block.gpsimd
        def _(pool):
            nc.gpsimd.memset(ident[:], 0.0).then_inc(consts, 1)
            pool.wait_ge(consts, 1)
            nc.gpsimd.affine_select(out=ident[:], in_=ident[:], compare_op=ALU.not_equal, fill=1.0,
                                    base=0, pattern=[[-1, P]], channel_multiplier=1).then_inc(consts, 1)
            nc.gpsimd.memset(minus_half, -0.5).then_inc(consts, 1)

            def split_lo(s, number):
                pool.wait_ge(hi_ready, number + 1)
                pool.wait_ge(lo_ready, number)
                nc.gpsimd.tensor_tensor(w_lo[:, s], w_raw[:, s], w_hi[:, s].bitcast(F32), ALU.subtract)\
                    .then_inc(lo_ready, 1)

            pool.wait_ge(cact_ready, 1)
            for k in range(KD):
                pool.wait_ge(first_full[k], 32)
                w, acc = ada_first[:, k, :, 0:POOL_K, :], acc_first[:, k]
                c3 = c_act[:, 0:POOL_K].rearrange("p (a k b) -> p a k b", a=1, b=1)
                nc.gpsimd.tensor_tensor(w, w, c3.to_broadcast([P, 2, POOL_K, P]), ALU.mult)\
                    .then_inc(pool_step, 1)
                for q in range(1, POOL_K):
                    pool.wait_ge(pool_step, k * POOL_K + q)
                    nc.gpsimd.tensor_tensor(acc, w[:, :, 0, :] if q == 1 else acc, w[:, :, q, :], ALU.add)\
                        .then_inc(pool_step, 1)

            split_lo(1, MIXIN + 1)
            pool.wait_ge(chunk_done, MIXIN)
            nc.gpsimd.memset(xa[:, :, 0:PAD], 0.0).then_inc(pads, 1)
            nc.gpsimd.memset(window[:, :, 0:PAD], 0.0).then_inc(pads, 1)
            pool.wait_ge(ws_full, 16)
            nc.gpsimd.affine_select(out=ws_raw[:], in_=ws_raw[:], compare_op=ALU.is_ge, fill=0.0,
                                    base=0, pattern=[[0, HEADS], [-1, P]], channel_multiplier=1)\
                .then_inc(ws_masked, 1)
            pool.wait_ge(ln_stat, NT)
            nc.gpsimd.tensor_scalar(rstd_in, mv[:, :, 1], EPS, 0.0, ALU.add, ALU.add).then_inc(ln_eps, 1)
            pool.wait_ge(ln_eps, 1)
            pool.wait_ge(consts, 3)
            nc.gpsimd.tensor_tensor(rstd, rstd_in, minus_half, ALU.pow).then_inc(ln_rstd, 1)
            link = 0
            for g, w in enumerate(POOL_WINDOWS):
                pool.wait_ge(xa_ready, g + 1)
                if g == 0:
                    pool.wait_ge(pads, 2)
                src, d, n = xa[:, g], 1, 0
                while d < w:
                    if g and n == 0:
                        pool.wait_ge(pooled_ready, g)
                    dst = window[:, n % 2]
                    ins = nc.gpsimd.tensor_tensor(dst[:, PAD:PAD + T], src[:, PAD:PAD + T],
                                                  src[:, PAD - d:PAD - d + T], ALU.add)
                    d *= 2
                    n += 1
                    src = dst
                    if d < w:
                        ins.then_inc(win_link, 1)
                        link += 1
                        pool.wait_ge(win_link, link)
                    else:
                        ins.then_inc(win_ready, 1)
            for s in range(2):
                split_lo(s, UP2 + s)

        @block.scalar
        def _(act):
            def split_hi(s, n, chunk):
                number, half = (chunk, chunk // 2) if isinstance(chunk, int) else chunk
                act.wait_ge(raw_full[s], half * 32 + 32)
                if not (isinstance(number, int) and number < 2):
                    act.wait_ge(chunk_done, number - 1)
                nc.scalar.copy(w_hi[:, s, 0:n], w_raw[:, s, 0:n]).then_inc(hi_ready, 1)

            def h_his(n, i0, i1):
                for i in range(i0, i1):
                    k, cols, half = STEPS[n][i]
                    act.wait_ge(scaled, H_AT[n] + i + 1)
                    nc.scalar.activation(h_hi[:, k, cols], work[:, SCALED[i % 4], cols], ACT.Identity,
                                         bias=mod_col(3 * n, k)).then_inc(h_hi_ready, 1)

            def root(n, half):
                act.wait_ge(sum_done, 2 * (n - 1) + half + 1)
                c = slice(half * NT // 2, (half + 1) * NT // 2)
                nc.scalar.activation(r_tok[:, c], ps[:, MOD, c], ACT.Sqrt, bias=eps_col,
                                     scale=1.0 / D).then_inc(root_ready, 1)

            def split_hi_part(s, part, number):
                if part == 0:
                    act.wait_ge(raw_full[s], number // 2 * 32 + 32)
                    act.wait_ge(chunk_done, number - 1)
                c = slice(part * FULL // 2, (part + 1) * FULL // 2)
                ins = nc.scalar.copy(w_hi[:, s, c], w_raw[:, s, c])
                ins.then_inc(hi_half if part == 0 else hi_ready, 1)

            act.wait_ge(dve_const, 2)
            for t in range(NT):
                act.wait_ge(x_full[t], 16)
                if t:
                    act.wait_ge(x_sq, t)
                nc.scalar.activation(work[:, 0:2, :].rearrange("p a t -> p (a t)"), x_tok[:, t, :], ACT.Square,
                                     accum_out=sum_tok[:, t:t + 1]).then_inc(x_sq, 1)
            act.wait_ge(vcol_ready, 1)
            nc.scalar.activation(c_act[:], vcol[:, rows["c"]:rows["c"] + KD], ACT.Silu).then_inc(cact_ready, 1)
            act.wait_ge(x_sq, NT)
            nc.scalar.activation(r_tok, sum_tok, ACT.Sqrt, bias=eps_col, scale=1.0 / D).then_inc(root_ready, 1)
            for k in range(1, KD, 2):
                act.wait_ge(x_T, k + 1)
                nc.scalar.copy(xT[:, k, :], ps[:, k % 4, :]).then_inc(x_odd, 1)
            for s in range(2):
                split_hi(s, FULL, s)
            h_his(0, 0, KD)

            def up_step(j, jn, s, n_next, nxt):
                act.wait_ge(chunk_done, nxt[0] - 1)
                if not (isinstance(jn, int) and jn == 0):
                    act.wait_ge(prod_ready, jn)
                nc.scalar.activation(work[:, 0, :], ps[:, 2 * s, :], ACT.Silu).then_inc(silu_ready, 1)
                if isinstance(jn, int) and jn == 0:
                    split_hi_part(s, 0, nxt[0])
                    split_hi_part(s, 1, nxt[0])
                else:
                    split_hi(s, n_next, nxt)
                act.wait_ge(prod_ready, jn + 1)
                nc.scalar.copy(a_hi[:, bass.ds(j, 1), :], work[:, 1:2, :]).then_inc(a_hi_ready, 1)

            def up(base, nth):
                for j in range(2):
                    up_step(j, j + nth * KF, j, FULL, (base + j + 2, base // 2 + 1))
                with act.Fori(1, KF // 2 - 1) as i:
                    for s in range(2):
                        up_step(i * 2 + s, i * 2 + (s + nth * KF), s, FULL,
                                (i * 2 + (s + base + 2), i + (base // 2 + 1)))
                for s in range(2):
                    j = KF - 2 + s
                    up_step(j, j + nth * KF, s, HALF, (base + j + 2, (base + j + 2) // 2))

            def square(m, x_count, added):
                act.wait_ge(x_new, x_count + 1)
                act.wait_ge(sq_added, added)
                src = xT[:, m, :] if isinstance(m, int) else xT[:, bass.ds(m, 1), :]
                dst = work[:, 0, :] if isinstance(m, int) else work[:, 0:1, :]
                nc.scalar.activation(dst, src, ACT.Square).then_inc(sq_ready, 1)

            def square_half(m, half, n, dst):
                cols = HALVES[half]
                act.wait_ge(last_new, n)
                nc.scalar.activation(work[:, dst, cols], xT[:, m, cols], ACT.Square).then_inc(last_sq, 1)

            def copy_out_half(half):
                act.wait_ge(out_T, KD + half)
                t0 = half * NT // 2
                src = ps[:, (SUM, 4)[half], 0:TH].rearrange("p (t f) -> p t f", f=P)
                nc.scalar.copy(out_tok[:, t0:t0 + NT // 2, (KD - 1) * P:D], src).then_inc(out_copied, 1)

            def finish(half):
                t = half * NT // 2 + 1
                act.wait_ge(r_ready, 6 + half)
                act.wait_ge(out_copied, KD + half)
                nc.scalar.activation(out_tok[:, t, :], out_tok[:, t, :], ACT.Copy,
                                     scale=r_tok[:, t:t + 1]).then_inc(y_out_act, 1)

            def copy_out(m):
                act.wait_ge(out_T, m + 1)
                src = ps[:, SUM, :].rearrange("p (t f) -> p t f", t=NT)
                nc.scalar.copy(out_tok[:, :, bass.ds(m * P, P)], src).then_inc(out_copied, 1)

            def down(base, x_count, sq_count, last):
                nc.scalar.activation(dummy, ones[:, 0:1], ACT.Sqrt)
                with act.Fori(0, KD - 1) as m:
                    for s in range(2):
                        split_hi(s, HALF, (m * 2 + (base + s + 2), m + (base // 2 + 1)))
                    square(m, m + x_count, m + (sq_count + 1))
                    if last:
                        copy_out(m)
                if not last:
                    split_hi(0, FULL, base + 2 * KD)
                act.wait_ge(sq_added, sq_count + KD)

            up(UP1, 0)
            down(DOWN1, X_AT[0], SQ_AT[0], False)
            square_half(KD - 1, 0, 1, 0)
            root(1, 0)
            h_his(1, 0, 2)
            square_half(KD - 1, 1, 2, 0)
            h_his(1, 2, 3)
            split_hi_part(1, 0, MIXIN + 1)
            h_his(1, 3, 4)
            root(1, 1)
            split_hi_part(1, 1, MIXIN + 1)
            h_his(1, 4, len(STEPS[1]))

            split_hi(0, FULL, MIXIN + 2)
            split_hi(1, FULL, MIXIN + 3)
            for t in range(NT):
                act.wait_ge(chunk_done, MIXIN + 2)
                nc.scalar.activation(v_tok[:, t, :], ps[:, t, :], ACT.Gelu_apprx_tanh).then_inc(v_gelu, 1)
            for q in range(2):
                act.wait_ge(ws_T, q + 1)
                nc.scalar.copy(wsT[:, 4 * q:4 * q + 4, :],
                               ps[:, 6 + q, :].rearrange("p (h t) -> p h t", h=4)).then_inc(ws_ready, 1)
            for q in range(2):
                act.wait_ge(chunk_done, MIXIN + 3 + q)
                for g in range(2):
                    nc.scalar.copy(xa[:, 2 * q + g, PAD:PAD + T], ps[:, (4, 5, 0, 1)[2 * q + g], :])\
                        .then_inc(xa_ready, 1)
                split_hi(q, FULL, MIXIN + 4 + q)
            for q in range(2):
                act.wait_ge(chunk_done, MIXIN + 5 + q)
                for g in range(2):
                    nc.scalar.activation(u_gelu[:, 2 * q + g, :], ps[:, (2, 3, 4, 5)[2 * q + g], :],
                                         ACT.Gelu_apprx_tanh).then_inc(u_ready, 1)
                if q == 0:
                    split_hi(0, FULL, MIXOUT)
            for g in range(KH):
                act.wait_ge(mixed, g + 1)
                nc.scalar.activation(y_hi[:, g, :], ps[:, (6, 7, 0, 1)[g], :], ACT.Identity,
                                     scale=vec("pool_scale", g)).then_inc(y_hi_ready, 1)
            split_hi(1, FULL, MIXOUT + 1)
            for g in range(KH):
                act.wait_ge(y32_ready, g + 1)
                nc.scalar.copy(y_hi[:, KH + g, :], pooled[:, g, :]).then_inc(y_hi_ready, 1)
            nc.scalar.activation(dummy, ones[:, 0:1], ACT.Sqrt)
            for q in range(KD // 2 - 1):
                if q < 2:
                    split_hi(q % 2, FULL, MIXOUT + 2 + q)
                for m in (2 * q, 2 * q + 1):
                    square(m, X_AT[1] + m, SQ_AT[1] + m + 1)
            split_hi(0, FULL, UP2)
            act.wait_ge(sq_added, SQ_AT[2])
            square_half(KD - 2, 0, LAST_AT[1] + 1, 2)
            square_half(KD - 1, 0, LAST_AT[1] + 2, 0)
            root(2, 0)
            square_half(KD - 2, 1, LAST_AT[1] + 3, 2)
            h_his(2, 0, 3)
            square_half(KD - 1, 1, LAST_AT[1] + 4, 0)
            h_his(2, 3, 6)
            root(2, 1)
            split_hi_part(1, 0, UP2 + 1)
            h_his(2, 6, 8)
            split_hi_part(1, 1, UP2 + 1)
            h_his(2, 8, len(STEPS[2]))

            up(UP2, 1)
            down(DOWN2, X_AT[2], SQ_AT[2], True)
            for half in range(2):
                square_half(KD - 1, half, LAST_AT[2] + half + 1, 0)
                copy_out_half(half)
                root(3, half)
                finish(half)

        @block.vector
        def _(dve):
            def split_lo(s, n, number):
                dve.wait_ge(hi_ready, number + 1)
                nc.vector.tensor_tensor(w_lo[:, s, 0:n], w_raw[:, s, 0:n], w_hi[:, s, 0:n].bitcast(F32),
                                        ALU.subtract).then_inc(lo_ready, 1)

            def split_lo_part(s, part, number):
                if part or number < 2:
                    dve.wait_ge(hi_ready, number + 1)
                else:
                    dve.wait_ge(hi_half, 1)
                c = slice(part * FULL // 2, (part + 1) * FULL // 2)
                ins = nc.vector.tensor_tensor(w_lo[:, s, c], w_raw[:, s, c], w_hi[:, s, c].bitcast(F32),
                                              ALU.subtract)
                ins.then_inc(lo_ready if part else lo_half, 1)

            def invert(n, r):
                dve.wait_ge(root_ready, n)
                nc.vector.reciprocal(r, r).then_inc(r_ready, 1)
                dve.wait_ge(r_ready, n)

            def diagonal(n, t0, t1):
                invert(n, r_tok[:, t0:t1])
                nc.vector.tensor_tensor(
                    work[:, 2, t0 * P:t1 * P].rearrange("p (t q) -> p t q", q=P),
                    ident[:].rearrange("p (a q) -> p a q", a=1).to_broadcast([P, t1 - t0, P]),
                    r_tok[:, t0:t1].rearrange("p (t a) -> p t a", a=1).to_broadcast([P, t1 - t0, P]), ALU.mult)\
                    .then_inc(diag_ready, 1)

            def scale_step(n, i):
                k, cols, half = STEPS[n][i]
                if i >= 4:
                    dve.wait_ge(h_ready, H_AT[n] + i - 3)
                dst, src = work[:, SCALED[i % 4], cols], xT[:, k, cols]
                if n == 0:
                    r = ps[:, SUM, :]
                elif half is not None:
                    r = ps[:, SPREAD[n][half], 0:TH]
                else:
                    b0, b1 = SPREAD[n]
                    r = ps[:, b0:b1 + 1:b1 - b0, 0:TH]
                    dst, src = (v.rearrange("p (a t) -> p a t", a=2) for v in (dst, src))
                nc.vector.scalar_tensor_tensor(dst, src, gs[:, n, k:k + 1], r, ALU.mult, ALU.mult)\
                    .then_inc(scaled, 1)

            def lo_step(n, i):
                k, cols, half = STEPS[n][i]
                dve.wait_ge(h_hi_ready, H_AT[n] + i + 1)
                nc.vector.scalar_tensor_tensor(
                    h_lo[:, k, cols], work[:, SCALED[i % 4], cols], mod_col(3 * n, k),
                    h_hi[:, k, cols].bitcast(F32), ALU.add, ALU.subtract).then_inc(h_ready, 1)

            def norm(n, i0, i1):
                def last_lo(i):
                    return len(STEPS[n]) - 1 if i == len(STEPS[n]) - 1 else i - (1 if i < LONG_LAG[n] else 2)

                for i in range(i0, i1):
                    scale_step(n, i)
                    for j in range(last_lo(i - 1) + 1 if i else 0, last_lo(i) + 1):
                        lo_step(n, j)

            def gains(n, name, scale_section):
                nc.vector.scalar_tensor_tensor(
                    gs[:, n, :], mod[:, scale_section * KD:(scale_section + 1) * KD], 1.0,
                    vcol[:, rows[name]:rows[name] + KD], ALU.add, ALU.mult).then_inc(mod_ready, 1)

            def take_mod(u0, u1, n):
                dve.wait_ge(ada_summed, n)
                c0, c1 = FIRST + 2 * u0, FIRST + 2 * u1
                for b in range(P // Q):
                    rows_b = slice(b * Q, (b + 1) * Q)
                    sums = ps[rows_b, MOD, 0:(c1 - c0) * (P // Q)].rearrange("p (c b) -> p c b", b=P // Q)
                    nc.vector.tensor_tensor(mod[rows_b, c0:c1], sums[:, :, b],
                                            vcol[rows_b, rows["b_ada"] + c0:rows["b_ada"] + c1], ALU.add)\
                        .then_inc(mod_link, 1)
                dve.wait_ge(mod_link, n * (P // Q))

            def ada_unit(u):
                for k in range(KD):
                    if not (isinstance(u, int) and u == 0 and k == 0):
                        dve.wait_ge(ada_link, u * LINKS + k)
                    if k % KA == 0:
                        dve.wait_ge(ada_full[k // KA], u * 16 + 16)
                    w = ada_raw[:, k // KA, k % KA, :]
                    if k == 0:
                        ins = nc.vector.tensor_scalar(ada_acc[:], w, c_act[:, 0:1], None, ALU.mult)
                    else:
                        ins = nc.vector.scalar_tensor_tensor(ada_acc[:], w, c_act[:, k:k + 1],
                                                             ada_acc[:], ALU.mult, ALU.add)
                    ins.then_inc(ada_link, 1)
                dve.wait_ge(ada_link, u * LINKS + KD)
                nc.vector.transpose(ada_T[:], ada_acc[:]).then_inc(ada_link, 1)
                dve.wait_ge(ada_link, u * LINKS + (KD + 1))
                dst = ada_part[:, u, :] if isinstance(u, int) else ada_part[:, bass.ds(u, 1), :]
                src = ada_T[:].rearrange("p (b q) -> p b q", q=Q)
                if not isinstance(u, int):
                    dst = dst.rearrange("p a b -> p (a b)")
                nc.vector.reduce_sum(dst, src, axis=mybir.AxisListType.X).then_inc(ada_link, 1)

            def up_step(j, jn, s, base, n_next, ada):
                first = isinstance(jn, int) and jn == 0
                if ada:
                    ada_unit(j)
                dve.wait_ge(silu_ready, jn + 1)
                if not first:
                    dve.wait_ge(a_ready, jn)
                nc.vector.tensor_tensor(work[:, 1, :], work[:, 0, :], ps[:, 2 * s + 1, :], ALU.mult)\
                    .then_inc(prod_ready, 1)
                if first:
                    for part in range(2):
                        split_lo_part(s, part, base + 2)
                else:
                    split_lo(s, n_next, j + (base + 2))
                dve.wait_ge(a_hi_ready, jn + 1)
                if isinstance(j, int):
                    dst, prod, hi = a_lo[:, j, :], work[:, 1, :], a_hi[:, j, :]
                else:
                    dst, prod, hi = a_lo[:, bass.ds(j, 1), :], work[:, 1:2, :], a_hi[:, bass.ds(j, 1), :]
                nc.vector.tensor_tensor(dst, prod, hi.bitcast(F32), ALU.subtract).then_inc(a_ready, 1)

            def up(base, nth, ada):
                if ada:
                    for s in range(2):
                        up_step(s, s, s, base, FULL, ada)
                with dve.Fori(1 if ada else 0, KF // 2 - 1) as i:
                    for s in range(2):
                        up_step(i * 2 + s, i * 2 + (s + nth * KF), s, base, FULL, ada)
                for s in range(2):
                    j = KF - 2 + s
                    up_step(j, j + nth * KF, s, base, HALF, ada)

            def update(m, n_mm, bank, gate, x_dst):
                dve.wait_ge(chunk_done, n_mm)
                nc.vector.scalar_tensor_tensor(x_dst, ps[:, bank:bank + 1, :], gate, x_dst,
                                               ALU.mult, ALU.add).then_inc(x_new, 1)

            def update_half(m, half, bank, gate):
                cols = HALVES[half]
                nc.vector.scalar_tensor_tensor(xT[:, m, cols], ps[:, bank, cols], gate, xT[:, m, cols],
                                               ALU.mult, ALU.add).then_inc(last_new, 1)

            def add_squares(sq_n):
                dve.wait_ge(sq_ready, sq_n)
                nc.vector.tensor_tensor(work[:, 1, :], work[:, 1, :], work[:, 0, :], ALU.add)\
                    .then_inc(sq_added, 1)

            def final_gain(m, x_count):
                dve.wait_ge(x_new, x_count + 1)
                if not (isinstance(m, int) and m == 0):
                    dve.wait_ge(out_T, m)
                if isinstance(m, int):
                    src, g = xT[:, m, :], vec("gfin", m)
                else:
                    src, g = xT[:, bass.ds(m, 1), :], vcol[:, bass.ds(m + rows["gfin"], 1)]
                dst = work[:, 2, :] if isinstance(m, int) else work[:, 2:3, :]
                nc.vector.tensor_scalar(dst, src, g, None, ALU.mult).then_inc(yg_scaled, 1)

            def finish(half):
                cols, n = HALVES[half], LAST_AT[2] + half + 1
                if half == 0:
                    dve.wait_ge(last_done, 5)
                else:
                    dve.wait_ge(chunk_done, END)
                update_half(KD - 1, half, LAST_BANK[half], half_gate[:, 1, KD - 1:KD])
                dve.wait_ge(last_new, n)
                dve.wait_ge(out_T, KD - 1)
                nc.vector.tensor_scalar(work[:, 2, cols], xT[:, KD - 1, cols], vec("gfin", KD - 1), None,
                                        ALU.mult).then_inc(yg_scaled, 1)
                t = half * NT // 2
                invert(6 + half, r_tok[:, t:t + NT // 2])
                dve.wait_ge(out_copied, KD + half)
                nc.vector.tensor_scalar(out_tok[:, t, :], out_tok[:, t, :], r_tok[:, t:t + 1], None, ALU.mult)\
                    .then_inc(y_out_dve, 1)

            def down(base, x_count, gate_n, ada, last):
                dve.wait_ge(a_ready, (gate_n + 1) * KF)
                nc.vector.memset(work[:, 1, :], 0.0).then_inc(sq_added, 1)

                def block_of(m, bank, unit):
                    if isinstance(m, int):
                        gate, x_dst = half_gate[:, gate_n, m:m + 1], xT[:, m:m + 1, :]
                    else:
                        gate, x_dst = half_gate[:, gate_n, bass.ds(m, 1)], xT[:, bass.ds(m, 1), :]
                    split_lo(0, HALF, m * 2 + (base + 2))
                    if unit is not None:
                        ada_unit(unit)
                    split_lo(1, HALF, m * 2 + (base + 3))
                    update(m, m * 2 + (base + 2), bank, gate, x_dst)
                    if last:
                        final_gain(m, m + x_count)
                    add_squares(m + (x_count + 1))

                pairs = (UNITS - KF) // 2 if ada else KD // 2 - 1
                if last:
                    for q in range(2):
                        block_of(q, 4 + q, None)
                with dve.Fori(1 if last else 0, pairs) as i:
                    for q in range(2):
                        block_of(i * 2 + q, 4 + q, i * 2 + (q + KF) if ada else None)
                for m in range(2 * pairs, KD - 1):
                    block_of(m, 4 + m % 2, None)

            nc.vector.memset(ones[:], 1.0).then_inc(dve_const, 1)
            nc.vector.memset(eps_col, EPS).then_inc(dve_const, 1)
            for t in range(PAD):
                nc.vector.memset(inv_count[:, t:t + 1], 1.0 / (t + 1)).then_inc(dve_const, 1)
            dve.wait_ge(dve_const, 2 + PAD)
            dve.wait_ge(consts, 2)
            nc.vector.reduce_sum(fold[:, 0:Q], ident[:].rearrange("p (b q) -> p q b", q=Q),
                                 axis=mybir.AxisListType.X).then_inc(dve_const, 1)
            dve.wait_ge(dve_const, 3 + PAD)
            for b in range(1, P // Q):
                nc.vector.tensor_copy(fold[:, b * Q:(b + 1) * Q], fold[:, 0:Q]).then_inc(dve_const, 1)
            dve.wait_ge(vec_T, 1)
            nc.vector.tensor_copy(vcol[:], ps[:, SUM, 0:NV]).then_inc(vcol_ready, 1)
            for k in range(0, KD, 2):
                dve.wait_ge(x_T, k + 1)
                nc.vector.tensor_copy(xT[:, k, :], ps[:, k % 4, :]).then_inc(x_even, 1)
            dve.wait_ge(cact_ready, 1)

            def first_sum(k):
                dve.wait_ge(first_full[k], 32)
                dve.wait_ge(pool_step, (k + 1) * POOL_K)
                for i in range(DVE_K):
                    if i:
                        dve.wait_ge(first_step, k * DVE_K + i)
                    q, acc = POOL_K + i, acc_first[:, k]
                    nc.vector.scalar_tensor_tensor(acc, ada_first[:, k, :, q, :], c_act[:, q:q + 1], acc,
                                                   ALU.mult, ALU.add).then_inc(first_step, 1)

            def first_block(k):
                def two(columns):
                    return columns.rearrange("p (s k) -> p s k", s=2)[:, :, k]

                bank = MOD if k % 2 == 0 else MOD_ODD
                dve.wait_ge(first_summed, k + 1)
                nc.vector.tensor_tensor(two(mod[:, 0:FIRST]), two(ps[:, bank, 0:FIRST]),
                                        two(vcol[:, rows["b_ada"]:rows["b_ada"] + FIRST]), ALU.add)\
                    .then_inc(first_taken, 1)
                dve.wait_ge(first_taken, k + 1)
                nc.vector.scalar_tensor_tensor(gs[:, 0, k:k + 1], mod_col(1, k), 1.0, vec("g1", k),
                                               ALU.add, ALU.mult).then_inc(first_gain, 1)
                dve.wait_ge(first_gain, k + 1)
                scale_step(0, k)

            first_sum(0)
            dve.wait_ge(consts, 2)
            diagonal(1, 0, NT)
            split_lo(0, FULL, 0)
            first_sum(1)
            dve.wait_ge(r_spread, 1)
            dve.wait_ge(x_even, KD // 2)
            dve.wait_ge(x_odd, KD // 2)
            first_block(0)
            split_lo_part(1, 0, 1)
            lo_step(0, 0)
            split_lo_part(1, 1, 1)
            for k in range(2, KD):
                first_sum(k)
                first_block(k - 1)
                if k > 2:
                    lo_step(0, k - 2)
            first_block(KD - 1)
            lo_step(0, KD - 2)
            lo_step(0, KD - 1)

            up(UP1, 0, True)
            take_mod(0, KF, 1)
            gains(1, "gmix", 4)
            nc.vector.tensor_scalar(half_gate[:, 0, :], mod[:, 2 * KD:3 * KD], HALF_STEP, None, ALU.mult)\
                .then_inc(mod_ready, 1)
            dve.wait_ge(mod_ready, 2)
            down(DOWN1, X_AT[0], 0, True, False)
            take_mod(KF, UNITS, 2)
            gains(2, "g2", 7)
            nc.vector.tensor_scalar(half_gate[:, 1, :], mod[:, 8 * KD:9 * KD], HALF_STEP, None, ALU.mult)\
                .then_inc(mod_ready, 1)
            dve.wait_ge(mod_ready, 4)
            split_lo(0, FULL, MIXIN)
            dve.wait_ge(last_done, 1)
            update_half(KD - 1, 0, LAST_BANK[0], half_gate[:, 0, KD - 1:KD])
            diagonal(2, 0, NT // 2)
            dve.wait_ge(r_spread, 2)
            norm(1, 0, 2)
            dve.wait_ge(chunk_done, MIXIN)
            update_half(KD - 1, 1, LAST_BANK[1], half_gate[:, 0, KD - 1:KD])
            norm(1, 2, 4)
            diagonal(3, NT // 2, NT)
            dve.wait_ge(r_spread, 3)
            norm(1, 4, len(STEPS[1]))

            dve.wait_ge(lo_ready, MIXIN + 2)
            for s in range(2):
                split_lo(s, FULL, MIXIN + 2 + s)
            for t in range(NT):
                dve.wait_ge(v_gelu, t + 1)
                nc.vector.bn_stats(stats[:, t, :], v_tok[:, t, :]).then_inc(ln_link, 1)
            for t in range(NT):
                dve.wait_ge(ln_link, t + 1)
                nc.vector.bn_aggr(mv[:, t, :], stats[:, t, :]).then_inc(ln_stat, 1)
            dve.wait_ge(ln_rstd, 1)
            for t in range(NT):
                nc.vector.tensor_scalar(v_tok[:, t, :], v_tok[:, t, :], mv[:, t, 0:1], rstd[:, t:t + 1],
                                        ALU.subtract, ALU.mult).then_inc(ln_link, 1)
            dve.wait_ge(mix_full, 16 * (3 + HEADS))
            for t in range(NT):
                dve.wait_ge(ln_link, NT + t + 1)
                nc.vector.tensor_tensor(v_tok[:, t, :], v_tok[:, t, :], ln_g[:], ALU.mult).then_inc(ln_link, 1)
            for t in range(NT):
                dve.wait_ge(ln_link, 2 * NT + t + 1)
                nc.vector.tensor_tensor(v_tok[:, t, :], v_tok[:, t, :], ln_b[:], ALU.add).then_inc(vn_ready, 1)
            split_lo(0, FULL, MIXIN + 4)
            for g, w in enumerate(POOL_WINDOWS):
                if g == 2:
                    split_lo(1, FULL, MIXIN + 5)
                dve.wait_ge(win_ready, g + 1)
                wsum = window[:, (w.bit_length() - 2) % 2]
                nc.vector.tensor_tensor(pooled[:, g, 0:w], wsum[:, PAD:PAD + w], inv_count[:, 0:w], ALU.mult)\
                    .then_inc(pooled_link, 1)
                nc.vector.scalar_tensor_tensor(pooled[:, g, w:T], wsum[:, PAD + w:PAD + T], 1.0 / w,
                                               xa[:, g, PAD + w:PAD + T], ALU.mult, ALU.subtract)\
                    .then_inc(pooled_link, 1)
                dve.wait_ge(pooled_link, 2 * g + 2)
                nc.vector.tensor_tensor(pooled[:, g, 0:w], pooled[:, g, 0:w], xa[:, g, PAD:PAD + w],
                                        ALU.subtract).then_inc(pooled_ready, 1)
            split_lo(0, FULL, MIXOUT)
            for g in range(KH):
                dve.wait_ge(y_hi_ready, g + 1)
                nc.vector.scalar_tensor_tensor(y_lo[:, g, :], ps[:, (6, 7, 0, 1)[g], :], vec("pool_scale", g),
                                               y_hi[:, g, :].bitcast(F32), ALU.mult, ALU.subtract)\
                    .then_inc(y_ready, 1)
            split_lo(1, FULL, MIXOUT + 1)
            for g in range(KH):
                dve.wait_ge(spatial, g + 1)
                dve.wait_ge(u_ready, g + 1)
                v3 = pooled[:, g, :].rearrange("p (n t) -> p n t", n=NT)
                sv3 = ps[:, (2, 3, 6, 7)[g], :].rearrange("p (n t) -> p n t", n=NT)
                b3 = bias_t[:, g:g + 1, :].to_broadcast([P, NT, P])
                nc.vector.tensor_tensor(v3, sv3, b3, ALU.add).then_inc(gate_link, 1)
                dve.wait_ge(gate_link, g + 1)
                nc.vector.tensor_tensor(pooled[:, g, :], pooled[:, g, :], u_gelu[:, g, :], ALU.mult)\
                    .then_inc(y32_ready, 1)
                if g:
                    dve.wait_ge(y_hi_ready, KH + g)
                    nc.vector.tensor_tensor(y_lo[:, KH + g - 1, :], pooled[:, g - 1, :],
                                            y_hi[:, KH + g - 1, :].bitcast(F32), ALU.subtract)\
                        .then_inc(y_ready, 1)
            dve.wait_ge(y_hi_ready, 2 * KH)
            nc.vector.tensor_tensor(y_lo[:, KD - 1, :], pooled[:, KH - 1, :],
                                    y_hi[:, KD - 1, :].bitcast(F32), ALU.subtract).then_inc(y_ready, 1)
            nc.vector.memset(work[:, 1, :], 0.0).then_inc(sq_added, 1)
            for q in range(KD // 2 - 1):
                if q < 2:
                    split_lo(q % 2, FULL, MIXOUT + 2 + q)
                for g in range(2):
                    m = 2 * q + g
                    update(m, MIXOUT + q + 1, 2 * (q % 2) + g, mod_col(5, m), xT[:, m:m + 1, :])
                    add_squares(X_AT[1] + m + 1)
            for g in range(2):
                dve.wait_ge(last_done, 2 + g)
                update_half(KD - 2 + g, 0, MIX_LAST[0][g], mod_col(5, KD - 2 + g))
            diagonal(4, 0, NT // 2)
            dve.wait_ge(last_done, 4)
            update_half(KD - 2, 1, MIX_LAST[1][0], mod_col(5, KD - 2))
            dve.wait_ge(r_spread, 4)
            norm(2, 0, 3)
            dve.wait_ge(chunk_done, UP2)
            update_half(KD - 1, 1, MIX_LAST[1][1], mod_col(5, KD - 1))
            norm(2, 3, 6)
            diagonal(5, NT // 2, NT)
            norm(2, 6, 8)
            dve.wait_ge(r_spread, 5)
            norm(2, 8, len(STEPS[2]))
            dve.wait_ge(lo_ready, UP2 + 2)

            up(UP2, 1, False)
            down(DOWN2, X_AT[2], 1, False, True)
            for half in range(2):
                finish(half)

        @block.tensor
        def _(pe):
            def product(dst, w_h, w_l, a_h, a_l, start, stop):
                nc.tensor.matmul(dst, w_h, a_h, start=start, stop=False)
                nc.tensor.matmul(dst, w_h, a_l, start=False, stop=False)
                return nc.tensor.matmul(dst, w_l, a_h, start=False, stop=stop)

            def pair(s, number, banks, src_hi, src_lo, wait_k=None):
                pe.wait_ge(lo_ready, number + 1)
                hi, lo = pair_view(w_hi, s), pair_view(w_lo, s)
                for k in range(KD):
                    if wait_k:
                        wait_k(k)
                    for g in range(2):
                        ins = product(ps[:, banks[g], :], hi[:, g, k, :], lo[:, g, k, :],
                                      src_hi[:, k, :], src_lo[:, k, :], k == 0, k == KD - 1)
                ins.then_inc(chunk_done, 1)

            def sum_units(u0, u1):
                pe.wait_ge(ada_link, u1 * LINKS)
                pe.wait_ge(dve_const, 2 + PAD + P // Q)
                nc.tensor.matmul(ps[:, MOD, 0:(u1 - u0) * UNIT // Q], fold[:],
                                 ada_part[:, u0:u1, :].rearrange("p u b -> p (u b)"), start=True, stop=True)\
                    .then_inc(ada_summed, 1)

            def up(base, nth):
                def step(j, s):
                    pe.wait_ge(prod_ready, j + (nth * KF - 1))
                    pair(s, j + base, (2 * s, 2 * s + 1), h_hi, h_lo)

                if nth == 1:
                    step(1, 1)
                else:
                    pe.wait_ge(prod_ready, 1)
                    hi, lo = pair_view(w_hi, 0), pair_view(w_lo, 0)
                    for g in range(2):
                        if g == 0:
                            pe.wait_ge(lo_half, 2)
                        else:
                            pe.wait_ge(lo_ready, 3)
                        for k in range(KD):
                            ins = product(ps[:, g, :], hi[:, g, k, :], lo[:, g, k, :], h_hi[:, k, :],
                                          h_lo[:, k, :], k == 0, k == KD - 1)
                    ins.then_inc(chunk_done, 1)
                    step(3, 1)
                with pe.Fori(2 - nth, KF // 2) as i:
                    for s in range(2):
                        step(i * 2 + s, s)

            def down(base, gate_n, x_count, sq_count, last, between):
                def block_of(m, bank):
                    if not (isinstance(m, int) and m < 2):
                        pe.wait_ge(x_new, m + (x_count - 1))
                    for s in range(2):
                        pe.wait_ge(lo_ready, m * 2 + (base + s + 1))
                        pe.wait_ge(a_ready, gate_n * KF + (KC if s == 0 else KF))
                        hi, lo = half_view(w_hi, s), half_view(w_lo, s)
                        for k in range(KC):
                            ins = product(ps[:, bank, :], hi[:, k, :], lo[:, k, :],
                                          a_hi[:, s * KC + k, :], a_lo[:, s * KC + k, :],
                                          s == 0 and k == 0, s == 1 and k == KC - 1)
                        ins.then_inc(chunk_done, 1)
                        if not last and s == 0 and isinstance(m, int) and m == 0:
                            sum_units(0, KF)
                        if last and s == 0 and not (isinstance(m, int) and m == 0):
                            transpose_out(m - 1)

                def half_block(s, half, between):
                    cols = HALVES[half]
                    hi, lo = half_view(w_hi, s), half_view(w_lo, s)
                    for k in range(KC):
                        if between:
                            between(k)
                        ins = product(ps[:, LAST_BANK[half], cols], hi[:, k, :], lo[:, k, :],
                                      a_hi[:, s * KC + k, cols], a_lo[:, s * KC + k, cols],
                                      s == 0 and k == 0, s == 1 and k == KC - 1)
                    return ins

                for m in range(2):
                    block_of(m, 4 + m)
                with pe.Fori(1, KD // 2 - 1) as i:
                    for q in range(2):
                        block_of(i * 2 + q, 4 + q)
                block_of(KD - 2, 4)
                pe.wait_ge(x_new, x_count + KD - 2)
                if not last:
                    sum_units(KF, UNITS)
                pe.wait_ge(lo_ready, base + 2 * KD - 1)
                half_block(0, 0, None)
                half_block(0, 1, None).then_inc(chunk_done, 1)
                if last:
                    transpose_out(KD - 2)
                else:
                    pe.wait_ge(mod_ready, 4)
                sum_blocks(sq_count + KD)
                pe.wait_ge(lo_ready, base + 2 * KD)
                half_block(1, 0, None).then_inc(last_done, 1)
                ins = half_block(1, 1, between)
                return ins

            def transpose_out(m):
                pe.wait_ge(yg_scaled, m + 1)
                if not (isinstance(m, int) and m == 0):
                    pe.wait_ge(out_copied, m)
                for t in range(NT):
                    ins = nc.tensor.transpose(ps[:, SUM, t * P:(t + 1) * P], work[:, 2, t * P:(t + 1) * P],
                                              ident[:])
                ins.then_inc(out_T, 1)

            def transpose_half(half):
                pe.wait_ge(yg_scaled, KD + half)
                pe.wait_ge(out_copied, KD - 1)
                for t in range(NT // 2):
                    c = half * TH + t * P
                    ins = nc.tensor.transpose(ps[:, (SUM, 4)[half], t * P:(t + 1) * P], work[:, 2, c:c + P],
                                              ident[:])
                ins.then_inc(out_T, 1)

            def sum_columns(src, t0, t1, start, stop):
                for t in range(t0, t1):
                    ins = nc.tensor.matmul(ps[:, MOD, t:t + 1], work[:, src, t * P:(t + 1) * P],
                                           ones[:, 0:1], start=start and t == t0, stop=stop and t == t1 - 1,
                                           skip_group_check=True)
                return ins

            def sum_blocks(added):
                pe.wait_ge(sq_added, added)
                sum_columns(1, 0, NT, True, False)

            def sum_last(n, half, srcs):
                pe.wait_ge(last_sq, LAST_SQ[n][half])
                if half:
                    pe.wait_ge(root_ready, 2 * n)
                for src in srcs:
                    ins = sum_columns(src, half * NT // 2, (half + 1) * NT // 2, False, src == srcs[-1])
                ins.then_inc(sum_done, 1)

            def spread(n, bank, cols):
                pe.wait_ge(diag_ready, n)
                nc.tensor.matmul(ps[:, bank, 0:cols.stop - cols.start], ones[:], work[:, 2, cols],
                                 start=True, stop=True).then_inc(r_spread, 1)

            def pair_half(s, number, k, g, bank, half, src_hi, src_lo):
                cols = HALVES[half]
                hi, lo = pair_view(w_hi, s), pair_view(w_lo, s)
                return product(ps[:, bank, cols], hi[:, g, k, :], lo[:, g, k, :], src_hi[:, k, cols],
                               src_lo[:, k, cols], k == 0, k == KD - 1)

            pe.wait_ge(consts, 2)
            pe.wait_ge(vec_full, 16 * len(rows))
            nc.tensor.transpose(ps[:, SUM, 0:NV], vrow[0:NV, :], ident[0:NV, 0:NV]).then_inc(vec_T, 1)
            for t in range(NT):
                pe.wait_ge(x_full[t], 16)
            pe.wait_ge(vcol_ready, 1)
            pe.wait_ge(dve_const, 1)
            for k in range(KD):
                if k >= 4:
                    pe.wait_ge(x_odd if k % 2 else x_even, (k - 4) // 2 + 1)
                for t in range(NT):
                    ins = nc.tensor.transpose(ps[:, k % 4, t * P:(t + 1) * P],
                                              x_tok[:, t, k * P:(k + 1) * P], ident[:])
                ins.then_inc(x_T, 1)
            pe.wait_ge(x_even, KD // 2)
            pe.wait_ge(x_odd, KD // 2)
            spread(1, SUM, slice(0, T))
            for k in range(KD + LAG):
                if k < KD:
                    bank = MOD if k % 2 == 0 else MOD_ODD
                    pe.wait_ge(first_full[k], 32)
                    if k >= 2:
                        pe.wait_ge(first_gain, k - 1)
                    for sec in range(2):
                        for q in range(POOL_K + DVE_K, KD):
                            nc.tensor.matmul(ps[:, bank, sec * KD + k:sec * KD + k + 1],
                                             ada_first[:, k, sec, q, :], c_act[:, q:q + 1],
                                             start=sec == 0 and q == POOL_K + DVE_K, stop=False,
                                             skip_group_check=True)
                    pe.wait_ge(first_step, (k + 1) * DVE_K)
                    for sec in range(2):
                        ins = nc.tensor.matmul(ps[:, bank, sec * KD + k:sec * KD + k + 1],
                                               acc_first[:, k, sec, :], ones[:, 0:1],
                                               start=False, stop=sec == 1, skip_group_check=True)
                    ins.then_inc(first_summed, 1)
                j = k - LAG
                if j >= 0:
                    pe.wait_ge(h_ready, j + 1)
                    for s in range(2):
                        pe.wait_ge(lo_ready, s + 1)
                        hi, lo = pair_view(w_hi, s), pair_view(w_lo, s)
                        for g in range(2):
                            ins = product(ps[:, 2 * s + g, :], hi[:, g, j, :], lo[:, g, j, :],
                                          h_hi[:, j, :], h_lo[:, j, :], j == 0, j == KD - 1)
                        if j == KD - 1:
                            ins.then_inc(chunk_done, 1)
            pe.wait_ge(first_gain, KD)

            up(UP1, 0)

            def beside(k):
                if k == 4:
                    sum_last(1, 0, (0,))
                if k == 8:
                    spread(2, SPREAD[1][0], HALVES[0])

            down(DOWN1, 0, X_AT[0], SQ_AT[0], False, beside).then_inc(chunk_done, 1)

            def v_tiles(s, k, t0, t1):
                hi, lo = v_view(w_hi, s), v_view(w_lo, s)
                ks = 4 * s + k
                for t in range(t0, t1):
                    ts = slice(t * P, (t + 1) * P)
                    first, final = ks == 0, ks == KD - 1
                    nc.tensor.matmul(ps[:, t, :], h_hi[:, ks, ts], hi[:, k, :], start=first, stop=False)
                    nc.tensor.matmul(ps[:, t, :], h_hi[:, ks, ts], lo[:, k, :], start=False, stop=False)
                    ins = nc.tensor.matmul(ps[:, t, :], h_lo[:, ks, ts], hi[:, k, :], start=False, stop=final)
                return ins

            pe.wait_ge(lo_ready, MIXIN + 1)
            for half in range(2):
                for k in range(KD // 2):
                    pe.wait_ge(h_ready, H_AT[1] + half * KD // 2 + k + 1)
                    ins = v_tiles(0, k, half * NT // 2, (half + 1) * NT // 2)
                    if half == 0 and k == 0:
                        sum_last(1, 1, (0,))
                    if half == 0 and k == 1:
                        spread(3, SPREAD[1][1], HALVES[1])
            ins.then_inc(chunk_done, 1)
            pe.wait_ge(lo_ready, MIXIN + 2)
            for k in range(KD // 2):
                pe.wait_ge(h_ready, H_AT[1] + KD + k + 1)
                ins = v_tiles(1, k, 0, NT)
            ins.then_inc(chunk_done, 1)
            pe.wait_ge(ws_masked, 1)
            for q in range(2):
                for h in range(4):
                    ins = nc.tensor.transpose(ps[:, 6 + q, h * P:(h + 1) * P], ws_raw[:, 4 * q + h, :],
                                              ident[:])
                ins.then_inc(ws_T, 1)
            pair(0, MIXIN + 2, (4, 5), h_hi, h_lo)
            pe.wait_ge(v_gelu, NT)
            pair(1, MIXIN + 3, (0, 1), h_hi, h_lo)
            pair(0, MIXIN + 4, (2, 3), h_hi, h_lo)
            pe.wait_ge(xa_ready, KH)
            pair(1, MIXIN + 5, (4, 5), h_hi, h_lo)
            pe.wait_ge(mix_full, 16 * (3 + HEADS))
            pe.wait_ge(ws_ready, 2)
            for g in range(KH):
                pe.wait_ge(pooled_ready, g + 1)
                nc.tensor.matmul(ps[:, (6, 7, 0, 1)[g], :], wp[:, g, :], pooled[:, g, :], start=True,
                                 stop=True).then_inc(mixed, 1)
            pe.wait_ge(vn_ready, NT)
            for g in range(KH):
                pe.wait_ge(u_ready if g < 2 else y_ready, 2)
                for n in range(NT):
                    for i in range(2):
                        h = 2 * g + i
                        ins = nc.tensor.matmul(
                            ps[i * HC:(i + 1) * HC, (2, 3, 6, 7)[g], n * P:(n + 1) * P],
                            v_tok[:, n, h * HC:(h + 1) * HC], wsT[:, h, :], start=True, stop=True)
                ins.then_inc(spatial, 1)

            def y_block(k):
                pe.wait_ge(y_ready, k + 1)

            for q in range(KD // 2):
                if q == 0:
                    pe.wait_ge(y_ready, KH)
                elif q == 1:
                    pe.wait_ge(y32_ready, 2)
                else:
                    pe.wait_ge(x_new, X_AT[1] + 2 * (q - 1))
                if q < KD // 2 - 1:
                    pair(q % 2, MIXOUT + q, (2 * (q % 2), 2 * (q % 2) + 1), y_hi, y_lo,
                         y_block if q == 0 else None)
            pe.wait_ge(lo_ready, UP2)
            for half in range(2):
                for g in range(2):
                    for k in range(KD):
                        if half == 1 and g == 0 and k == 1:
                            sum_blocks(SQ_AT[2])
                        if half == 1 and g == 0 and k == 5:
                            sum_last(2, 0, (2, 0))
                        if half == 1 and g == 1 and k == 0:
                            spread(4, SPREAD[2][0], HALVES[0])
                        ins = pair_half(1, UP2 - 1, k, g, MIX_LAST[half][g], half, y_hi, y_lo)
                    if not (half and g):
                        ins.then_inc(last_done, 1)
            ins.then_inc(chunk_done, 1)
            pe.wait_ge(x_new, X_AT[2])
            pe.wait_ge(lo_ready, UP2 + 1)
            for half in range(2):
                for k in range(KD):
                    pe.wait_ge(h_ready, H_AT[2] + half * KD + k + 1)
                    for g in range(2):
                        ins = pair_half(0, UP2, k, g, g, half, h_hi, h_lo)
                    if half == 0 and k == 1:
                        sum_last(2, 1, (2, 0))
                    if half == 0 and k == 4:
                        spread(5, SPREAD[2][1], HALVES[1])
            ins.then_inc(chunk_done, 1)

            up(UP2, 1)

            def transposes(k):
                if k == 5:
                    transpose_half(0)
                    sum_last(3, 0, (0,))

            down(DOWN2, 1, X_AT[2], SQ_AT[2], True, transposes).then_inc(chunk_done, 1)
            transpose_half(1)
            sum_last(3, 1, (0,))


_INS = ["x", "c", "w_ada", "b_ada", "norm_ffn1_g", "ffn1_w_in", "ffn1_w_out", "norm_mix_g", "w_mix_in",
        "w_pool", "pool_scale", "gmlp_ln_g", "gmlp_ln_b", "w_spatial", "b_spatial", "w_mix_out",
        "norm_ffn2_g", "ffn2_w_in", "ffn2_w_out", "norm_final_g"]


def kernel(**inputs):
    import numpy as _np
    import concourse.bacc as _bacc
    from concourse import mybir as _mybir
    from concourse.bass_utils import run_bass_kernel_spmd as _run

    nc = _bacc.Bacc("TRN2", target_bir_lowering=False, num_devices=1)
    arrays, args = {}, []
    for name in _INS:
        a = _np.ascontiguousarray(inputs[name])
        arrays[f"in_{name}_dram"] = a
        args.append(nc.dram_tensor(f"in_{name}_dram", a.shape, _mybir.dt.from_np(a.dtype),
                                   kind="ExternalInput").ap())
    x = inputs["x"]
    args.append(nc.dram_tensor("out_dram", x.shape, _mybir.dt.from_np(_np.dtype(x.dtype)),
                               kind="ExternalOutput").ap())
    build_program(nc, *args)
    r = _run(nc, [arrays], core_ids=[0])
    return r.results[0]["out_dram"]
```
